# Optimizing a Trainium2 kernel written in Bass

```python
import math
import jax, jax.numpy as jnp
from jax import lax
import numpy as np

D_MODEL = 1024
BATCH = 1
SEQ = 128
DEPTH = 1
DEC_BATCH = 1
DEC_SEQ = 1024
PAST_LEN = 256

GRID_W = 64
MIX_WIDTH = D_MODEL
GM_HEADS = 4
GM_HEAD_DIM = 128
GM_WIDTH = GM_HEADS * GM_HEAD_DIM
GM_CHUNK = 128
DN_HEADS = 4
DN_HEAD_K = 128
DN_HEAD_V = 128
DN_WIDTH = DN_HEADS * DN_HEAD_V
DN_QKV = 2 * DN_HEADS * DN_HEAD_K + DN_HEADS * DN_HEAD_V
DN_DIRS = 2
DN_CHUNK = 64
DN_CONV = 3
ROPE_BASE = 10000.0
IN_COLS = 2 * GM_WIDTH + DN_QKV + DN_WIDTH + 2 * DN_DIRS * DN_HEADS
IN_SPLITS = (GM_WIDTH, 2 * GM_WIDTH, 2 * GM_WIDTH + DN_QKV, 2 * GM_WIDTH + DN_QKV + DN_WIDTH,
             2 * GM_WIDTH + DN_QKV + DN_WIDTH + DN_DIRS * DN_HEADS)
PEER_HEADS = 8
PEER_NKEYS = 128
PEER_N = PEER_NKEYS * PEER_NKEYS
PEER_DKEY = 256
PEER_TOPK = 16
PEER_BLOCK = 128
EPS = 1e-6

kernel_name = "hymba_gmlp_gdn_peer_diffusion_step"

def rms_norm(x, gain):
    xf = x.astype(jnp.float32)
    y = xf * lax.rsqrt(jnp.mean(xf * xf, axis=-1, keepdims=True) + EPS)
    return (y * gain.astype(jnp.float32)).astype(x.dtype)

def l2_norm(x):
    return x * lax.rsqrt(jnp.sum(x * x, axis=-1, keepdims=True) + EPS)

def chunk_spatial_gate(u, v, ws, bs):
    B, L, H, dh = v.shape
    n = L // GM_CHUNK
    vf = v.astype(jnp.float32)
    vf = vf * lax.rsqrt(jnp.mean(vf * vf, axis=-1, keepdims=True) + EPS)
    vc = vf.reshape(B, n, GM_CHUNK, H, dh)
    s = jnp.einsum('hij,bnjhd->bnihd', ws.astype(jnp.float32), vc) + bs.astype(jnp.float32).T[None, None, :, :, None]
    return (u.astype(jnp.float32) * s.reshape(B, L, H, dh)).astype(u.dtype)

def short_conv(x, w):
    C = x.shape[-1]
    pad = DN_CONV // 2
    return lax.conv_general_dilated(x, w[:, None, :].astype(x.dtype), window_strides=(1,),
                                    padding=((pad, pad),), dimension_numbers=('NWC', 'WIO', 'NWC'),
                                    feature_group_count=C)

def grid_rope(x):
    L = x.shape[1]
    rows = L // GRID_W
    r, cidx = jnp.meshgrid(jnp.arange(rows), jnp.arange(GRID_W), indexing='ij')
    half = DN_HEAD_K // 2
    quarter = half // 2
    inv = ROPE_BASE ** (-jnp.arange(quarter, dtype=jnp.float32) / quarter)
    ang_r = r.reshape(-1).astype(jnp.float32)[:, None] * inv
    ang_c = cidx.reshape(-1).astype(jnp.float32)[:, None] * inv

    def rot(xh, ang):
        x1, x2 = xh[..., :quarter], xh[..., quarter:]
        cos = jnp.cos(ang)[None, :, None, :]
        sin = jnp.sin(ang)[None, :, None, :]
        return jnp.concatenate([x1 * cos - x2 * sin, x1 * sin + x2 * cos], axis=-1)

    return jnp.concatenate([rot(x[..., :half], ang_r), rot(x[..., half:], ang_c)], axis=-1)

def gated_delta_chunked(q, k, v, g, beta, s0):
    B, L, H, K = q.shape
    V = v.shape[-1]
    C = DN_CHUNK
    n = L // C

    def blk(t):
        t = t.reshape(B, n, C, H, *t.shape[3:])
        return jnp.moveaxis(t, 3, 1)

    qc, kc, vc, gc, bc = blk(q), blk(k), blk(v), blk(g), blk(beta)
    gcum = jnp.cumsum(gc, axis=-1)
    idx = jnp.arange(C)
    causal = idx[:, None] >= idx[None, :]
    strict = idx[:, None] > idx[None, :]
    decay = jnp.exp(jnp.where(causal, gcum[..., :, None] - gcum[..., None, :], -jnp.inf))
    kb = kc * bc[..., None]
    a = jnp.where(strict, jnp.einsum('bhnik,bhnjk->bhnij', kb, kc) * decay, 0.0)
    eye = jnp.eye(C, dtype=q.dtype)
    lhs = a + eye
    t_inv = lax.linalg.triangular_solve(lhs, jnp.broadcast_to(eye, lhs.shape), left_side=True, lower=True)
    w = jnp.einsum('bhnij,bhnjk->bhnik', t_inv, kb * jnp.exp(gcum)[..., None])
    u = jnp.einsum('bhnij,bhnjv->bhniv', t_inv, vc * bc[..., None])
    attn = jnp.einsum('bhnik,bhnjk->bhnij', qc, kc) * decay
    q_dec = qc * jnp.exp(gcum)[..., None]
    k_dec = kc * jnp.exp(gcum[..., -1:] - gcum)[..., None]
    g_last = jnp.exp(gcum[..., -1])

    def step(s, xs):
        w_i, u_i, attn_i, qd_i, kd_i, gl_i = xs
        v_new = u_i - jnp.einsum('bhck,bhkv->bhcv', w_i, s)
        o = jnp.einsum('bhck,bhkv->bhcv', qd_i, s) + jnp.einsum('bhij,bhjv->bhiv', attn_i, v_new)
        s = s * gl_i[..., None, None] + jnp.einsum('bhck,bhcv->bhkv', kd_i, v_new)
        return s, o

    xs = tuple(jnp.moveaxis(t, 2, 0) for t in (w, u, attn, q_dec, k_dec, g_last))
    s_final, o = lax.scan(step, s0, xs)
    o = jnp.transpose(o, (1, 0, 3, 2, 4)).reshape(B, L, H, V)
    return o, s_final

def deltanet_mixer(p_qkv, p_z, p_a, p_b, conv_w, a_log, dt_bias, norm_w, s0, use_rope):
    B, L, _ = p_qkv.shape
    qkv = jax.nn.silu(short_conv(p_qkv, conv_w)).astype(jnp.float32)
    q, k, v = jnp.split(qkv, [DN_HEADS * DN_HEAD_K, 2 * DN_HEADS * DN_HEAD_K], axis=-1)
    q = l2_norm(q.reshape(B, L, DN_HEADS, DN_HEAD_K))
    k = l2_norm(k.reshape(B, L, DN_HEADS, DN_HEAD_K))
    if use_rope:
        q = grid_rope(q)
        k = grid_rope(k)
    q = q * (DN_HEAD_K ** -0.5)
    v = v.reshape(B, L, DN_HEADS, DN_HEAD_V)
    a = p_a.astype(jnp.float32).reshape(B, L, DN_DIRS, DN_HEADS)
    b = p_b.astype(jnp.float32).reshape(B, L, DN_DIRS, DN_HEADS)
    g = -jnp.exp(a_log.astype(jnp.float32)) * jax.nn.softplus(a + dt_bias.astype(jnp.float32))
    beta = jax.nn.sigmoid(b)
    s0 = s0.astype(jnp.float32)
    o_f, s_f = gated_delta_chunked(q, k, v, g[:, :, 0], beta[:, :, 0], s0[:, 0])
    flip = lambda t: t[:, ::-1]
    o_b, s_b = gated_delta_chunked(flip(q), flip(k), flip(v), flip(g[:, :, 1]), flip(beta[:, :, 1]), s0[:, 1])
    o = o_f + flip(o_b)
    z = p_z.astype(jnp.float32).reshape(B, L, DN_HEADS, DN_HEAD_V)
    o = rms_norm(o, norm_w) * jax.nn.silu(z)
    return o.reshape(B, L, DN_WIDTH).astype(p_qkv.dtype), jnp.stack([s_f, s_b], axis=1)

def peer_ffn(h, wq, keys, u_tab, v_tab):
    B, L, D = h.shape
    hb = h.reshape(-1, PEER_BLOCK, D)

    def block(xb):
        T = xb.shape[0]
        q = (xb @ wq).reshape(T, PEER_HEADS, 2, PEER_DKEY // 2)
        s = jnp.einsum('thpk,hpnk->thpn', q, keys).astype(jnp.float32)
        sv, si = lax.top_k(s, PEER_TOPK)
        cand = (sv[:, :, 0, :, None] + sv[:, :, 1, None, :]).reshape(T, PEER_HEADS, PEER_TOPK * PEER_TOPK)
        cv, ci = lax.top_k(cand, PEER_TOPK)
        i1 = jnp.take_along_axis(si[:, :, 0], ci // PEER_TOPK, axis=-1)
        i2 = jnp.take_along_axis(si[:, :, 1], ci % PEER_TOPK, axis=-1)
        e = (i1 * PEER_NKEYS + i2).reshape(T, PEER_HEADS * PEER_TOPK)
        gate = jax.nn.softmax(cv, axis=-1).reshape(T, PEER_HEADS * PEER_TOPK)
        act = jax.nn.gelu(jnp.einsum('ted,td->te', u_tab[e], xb).astype(jnp.float32))
        coef = (gate * act).astype(xb.dtype)
        return jnp.einsum('te,ted->td', coef, v_tab[e])

    return lax.map(block, hb).reshape(B, L, D)

def trunk_layer(x, mod, s0, use_rope, w_in, w_out, g_pre_mix, g_post_mix, g_pre_ffn, g_post_ffn,
                gm_ws, gm_bs, dn_conv, dn_a_log, dn_dt_bias, dn_norm, peer_wq, peer_keys, peer_u, peer_v):
    B, L, _ = x.shape
    shift1, scale1, gate1, shift2, scale2, gate2 = jnp.split(mod, 6, axis=-1)
    h = rms_norm(x, g_pre_mix) * (1 + scale1) + shift1
    p = h @ w_in
    p_gu, p_gv, p_qkv, p_z, p_a, p_b = jnp.split(p, IN_SPLITS, axis=-1)
    gu = jax.nn.gelu(p_gu).reshape(B, L, GM_HEADS, GM_HEAD_DIM)
    gv = jax.nn.gelu(p_gv).reshape(B, L, GM_HEADS, GM_HEAD_DIM)
    o_a = chunk_spatial_gate(gu, gv, gm_ws, gm_bs).reshape(B, L, GM_WIDTH)
    o_b, s_new = deltanet_mixer(p_qkv, p_z, p_a, p_b, dn_conv, dn_a_log, dn_dt_bias, dn_norm, s0, use_rope)
    y = jnp.concatenate([o_a, o_b], axis=-1) @ w_out
    x = x + gate1 * rms_norm(y, g_post_mix)
    h2 = rms_norm(x, g_pre_ffn) * (1 + scale2) + shift2
    x = x + gate2 * rms_norm(peer_ffn(h2, peer_wq, peer_keys, peer_u, peer_v), g_post_ffn)
    return x, s_new

def setup_inputs(seed: int = 0) -> dict:
    key = jax.random.key(seed)
    ks = jax.random.split(key, 24)
    f32 = jnp.float32
    nrm = lambda k, shape, s: jax.random.normal(k, shape, f32) * s
    x_prompt = nrm(ks[0], (BATCH, SEQ, D_MODEL), 1.0)
    x_sample = nrm(ks[1], (DEC_BATCH, DEC_SEQ, D_MODEL), 1.0)
    state_delta = nrm(ks[2], (DEC_BATCH, DEPTH, DN_DIRS, DN_HEADS, DN_HEAD_K, DN_HEAD_V), DN_HEAD_K ** -0.5)
    c = nrm(ks[3], (DEC_BATCH, D_MODEL), 1.0)
    c_ctx = nrm(ks[4], (D_MODEL,), 1.0)
    w_mod = nrm(ks[5], (DEPTH, D_MODEL, 6 * D_MODEL), 0.5 * D_MODEL ** -0.5)
    b_mod = nrm(ks[6], (DEPTH, 6 * D_MODEL), 0.02)
    g_pre_mix = 1.0 + nrm(ks[7], (DEPTH, D_MODEL), 0.02)
    g_post_mix = 1.0 + nrm(ks[8], (DEPTH, D_MODEL), 0.02)
    g_pre_ffn = 1.0 + nrm(ks[9], (DEPTH, D_MODEL), 0.02)
    g_post_ffn = 1.0 + nrm(ks[10], (DEPTH, D_MODEL), 0.02)
    w_in = nrm(ks[11], (DEPTH, D_MODEL, IN_COLS), D_MODEL ** -0.5)
    w_out = nrm(ks[12], (DEPTH, MIX_WIDTH, D_MODEL), MIX_WIDTH ** -0.5)
    gm_ws = nrm(ks[13], (DEPTH, GM_HEADS, GM_CHUNK, GM_CHUNK), GM_CHUNK ** -0.5)
    gm_bs = 1.0 + nrm(ks[14], (DEPTH, GM_HEADS, GM_CHUNK), 0.02)
    dn_conv = nrm(ks[15], (DEPTH, DN_CONV, DN_QKV), DN_CONV ** -0.5)
    dn_a_log = jnp.log(jax.random.uniform(ks[16], (DEPTH, DN_DIRS, DN_HEADS), f32, 1.0, 16.0))
    dt = jnp.exp(jax.random.uniform(ks[17], (DEPTH, DN_DIRS, DN_HEADS), f32, math.log(1e-3), math.log(1e-1)))
    dn_dt_bias = dt + jnp.log(-jnp.expm1(-dt))
    dn_norm = 1.0 + nrm(ks[18], (DEPTH, DN_HEAD_V), 0.02)
    peer_wq = nrm(ks[19], (DEPTH, D_MODEL, PEER_HEADS * PEER_DKEY), D_MODEL ** -0.5)
    peer_keys = nrm(ks[20], (DEPTH, PEER_HEADS, 2, PEER_NKEYS, PEER_DKEY // 2), (PEER_DKEY // 2) ** -0.5)
    peer_u = nrm(ks[21], (DEPTH, PEER_N, D_MODEL), D_MODEL ** -0.5)
    peer_v = nrm(ks[22], (DEPTH, PEER_N, D_MODEL), D_MODEL ** -0.5)
    return {"x_prompt": x_prompt, "x_sample": x_sample, "state_delta": state_delta, "c": c, "c_ctx": c_ctx,
            "w_mod": w_mod, "b_mod": b_mod, "g_pre_mix": g_pre_mix, "g_post_mix": g_post_mix,
            "g_pre_ffn": g_pre_ffn, "g_post_ffn": g_post_ffn, "w_in": w_in, "w_out": w_out,
            "gm_ws": gm_ws, "gm_bs": gm_bs, "dn_conv": dn_conv, "dn_a_log": dn_a_log, "dn_dt_bias": dn_dt_bias,
            "dn_norm": dn_norm, "peer_wq": peer_wq, "peer_keys": peer_keys, "peer_u": peer_u, "peer_v": peer_v}

def reference(x_prompt, x_sample, state_delta, c, c_ctx, w_mod, b_mod, g_pre_mix, g_post_mix, g_pre_ffn,
              g_post_ffn, w_in, w_out, gm_ws, gm_bs, dn_conv, dn_a_log, dn_dt_bias, dn_norm, peer_wq, peer_keys,
              peer_u, peer_v):
    xp = x_prompt
    xs = x_sample
    new_states = []
    for l in range(DEPTH):
        mod_ctx = (jax.nn.silu(c_ctx) @ w_mod[l] + b_mod[l])[None, None, :]
        mod_lat = (jax.nn.silu(c) @ w_mod[l] + b_mod[l])[:, None, :]
        lw = (w_in[l], w_out[l], g_pre_mix[l], g_post_mix[l], g_pre_ffn[l], g_post_ffn[l], gm_ws[l], gm_bs[l],
              dn_conv[l], dn_a_log[l], dn_dt_bias[l], dn_norm[l], peer_wq[l], peer_keys[l], peer_u[l], peer_v[l])
        s0_ctx = jnp.zeros((xp.shape[0], DN_DIRS, DN_HEADS, DN_HEAD_K, DN_HEAD_V), jnp.float32)
        xp, s_ctx = trunk_layer(xp, mod_ctx, s0_ctx, False, *lw)
        xs, _ = trunk_layer(xs, mod_lat, state_delta[:, l], True, *lw)
        new_states.append(s_ctx.astype(x_prompt.dtype))
    new_state_delta = jnp.stack(new_states, axis=1)
    return (xp, xs, new_state_delta)


_drawn_inputs = setup_inputs


def setup_inputs(seed=0):
    import zlib

    import numpy as np

    out = dict(_drawn_inputs(seed))
    spreads = {}
    factors = {'state_delta': 2.738, 'g_post_ffn': 8.0, 'gm_bs': 3.522, 'dn_norm': 3.403}
    for name, (base, spread) in spreads.items():
        noise = np.random.default_rng([zlib.crc32(name.encode()), seed]).standard_normal(out[name].shape)
        drawn = base * np.exp(spread * noise) if base else spread * noise
        out[name] = __import__('jax').numpy.asarray(drawn.astype(out[name].dtype))
    for name, factor in factors.items():
        out[name] = (out[name] * factor).astype(out[name].dtype)
    return out
```

```python
from contextlib import ExitStack

import concourse.bass as bass
import numpy as np
from concourse import mybir

ALU = mybir.AluOpType
ACT = mybir.ActivationFunctionType
F32 = mybir.dt.float32
F32R = mybir.dt.float32r
U32 = mybir.dt.uint32
AX = mybir.AxisListType

P = 128
D = 1024
KB = D // P
TILES = 9
T = TILES * P
TC = 384
NTC = T // TC
HEADS = 4
HW = HEADS * P
UNITS = 8
GROUPS = 2
EPS = 1e-6
PH = 8
TOPK = 16
SLOTS = PH * TOPK
LEVELS = 7
FAR = -1e30
LOWEST = -3.0e38


def group_of(tile):
    return 0 if tile == 0 else 1


class Core:

    def __init__(self, nc, dram, stack):
        self.nc = nc
        self.dram = dram
        self.stack = stack

    def keep(self, name, shape, dt=F32):
        return self.stack.enter_context(self.nc.sbuf_tensor(name, shape, dt))


class Stage:

    def __init__(self, core, name):
        self.nc, self.name, self.stack = core.nc, name, ExitStack()

    def sb(self, name, shape, dt=F32):
        return self.stack.enter_context(self.nc.sbuf_tensor(f"{self.name}_{name}", shape, dt))

    def psum(self, name, shape, dt=F32):
        return self.stack.enter_context(self.nc.psum_tensor(f"{self.name}_{name}", shape, dt))

    def sem(self, name):
        return self.stack.enter_context(self.nc.semaphore(f"{self.name}_{name}"))

    def block(self):
        return self.stack.enter_context(self.nc.Block())

    def __enter__(self):
        return self

    def __exit__(self, *e):
        self.stack.close()


class Chain:

    def __init__(self, engine, sem):
        self.engine, self.sem, self.n = engine, sem, 0

    def __call__(self, ins):
        self.n += 1
        ins.then_inc(self.sem, 1)
        self.engine.wait_ge(self.sem, self.n)


def stage_modulation(core):
    nc, dram = core.nc, core.dram
    CW = 512
    NCH = 6 * D // CW
    BPC = CW // P
    SHIFT1, SCALE1, GATE1, SHIFT2, SCALE2, GATE2 = range(6)
    per = D // CW
    parts = [ch // per for ch in range(NCH)]
    col_chunks = [ch for ch in range(NCH) if parts[ch] not in (GATE1, GATE2)]
    gate_chunks = [ch for ch in range(NCH) if parts[ch] in (GATE1, GATE2)]
    with Stage(core, "mod") as st:
        ring = [st.sb(f"w{i}", [P, KB, CW]) for i in range(3)]
        ccol = st.sb("ccol", [P, KB, GROUPS])
        cact = st.sb("cact", [P, KB, GROUPS])
        cwide = st.sb("cwide", [P, GROUPS, KB, P])
        bcol = st.sb("bcol", [P, 6 * KB])
        gpre = st.sb("gpre", [P, 2, KB])
        brow = st.sb("brow", [P, 2, D])
        gpost = st.sb("gpost", [P, 2, D])
        gate_rows = st.sb("gate_rows", [P, 2, GROUPS, D])
        mcol = st.sb("mcol", [P, 6 * KB, GROUPS])
        pcol = st.psum("pcol", [P, 512])
        prow = [st.psum(f"prow{i}", [P, 512]) for i in range(4)]
        small_in = st.sem("small_in")
        w_in = [st.sem(f"w_in{i}") for i in range(3)]
        act_done = st.sem("act_done")
        wide_done = st.sem("wide_done")
        cols_used = st.sem("cols_used")
        rows_done = st.sem("rows_done")
        rows_read = st.sem("rows_read")
        dve_chain = st.sem("dve_chain")
        rows_out = st.sem("rows_out")
        pool_chain = st.sem("pool_chain")
        block = st.block()
        order = gate_chunks + col_chunks

        @block.sync
        def _(sp):
            sp.dma_start(ccol[:], dram["c_cols"]).then_inc(small_in, 16)
            sp.dma_start(bcol[:], dram["b_mod_cols"]).then_inc(small_in, 16)
            sp.dma_start(gpre[:], dram["g_pre_cols"]).then_inc(small_in, 16)
            sp.dma_start(brow[:], dram["b_gate_rows"].to_broadcast([P, 2, D])).then_inc(small_in, 16)
            sp.dma_start(gpost[:], dram["g_post_rows"].to_broadcast([P, 2, D])).then_inc(small_in, 16)
            sp.dma_start(core.tri[:], dram["tri"]).then_inc(small_in, 16)
            for n, ch in enumerate(order):
                old = n - 3
                if 0 <= old < len(gate_chunks):
                    sp.wait_ge(rows_done, GROUPS * (old + 1))
                elif old >= 0:
                    sp.wait_ge(cols_used, old - len(gate_chunks) + 1)
                sp.dma_start(ring[n % 3][:], dram["w_mod"][:, :, ch * CW:(ch + 1) * CW]).then_inc(w_in[n % 3], 16)

        @block.scalar
        def _(act):
            act.wait_ge(small_in, 6 * 16)
            nc.scalar.activation(cact[:], ccol[:], ACT.Silu).then_inc(act_done, 1)

        @block.gpsimd
        def _(pool):
            link = Chain(pool, pool_chain)
            link(nc.gpsimd.memset(core.ones[:], 1.0))
            link(nc.gpsimd.memset(core.ident[:], 0.0))
            link(nc.gpsimd.affine_select(out=core.ident[:], in_=core.ident[:], compare_op=ALU.not_equal, fill=1.0,
                                         base=0, pattern=[[-1, P]], channel_multiplier=1))
            pool.wait_ge(dve_chain, GROUPS * len(gate_chunks))
            pool.dma_start(dram["gate_rows"].rearrange("w p g d -> p w g d"), gate_rows[:]).then_inc(rows_out, 16)
            pool.wait_ge(rows_out, 16)

        @block.vector
        def _(dve):
            dve.wait_ge(act_done, 1)
            for g in range(GROUPS):
                for k in range(KB):
                    src = cact[:, k, g:g + 1].to_broadcast([P, P])
                    nc.vector.tensor_copy(cwide[:, g, k, :], src).then_inc(wide_done, 1)
            link = Chain(dve, dve_chain)
            for n, ch in enumerate(gate_chunks):
                which = 0 if parts[ch] == GATE1 else 1
                at = (ch % per) * CW
                for g in range(GROUPS):
                    dst = gate_rows[:, which, g, at:at + CW]
                    dve.wait_ge(rows_done, n * GROUPS + g + 1)
                    ins = nc.vector.tensor_tensor(dst, prow[(n * GROUPS + g) % 4][:], brow[:, which, at:at + CW], ALU.add)
                    ins.then_inc(rows_read, 1)
                    dve.wait_ge(rows_read, n * GROUPS + g + 1)
                    link(nc.vector.tensor_tensor(dst, dst, gpost[:, which, at:at + CW], ALU.mult))
            dve.wait_ge(cols_used, len(col_chunks))
            for part in (SHIFT1, SCALE1, SHIFT2, SCALE2):
                b = slice(part * KB, (part + 1) * KB)
                src = pcol[:, part * KB * GROUPS:(part + 1) * KB * GROUPS].rearrange("p (k g) -> p k g", g=GROUPS)
                bias = bcol[:, b].unsqueeze(2).to_broadcast([P, KB, GROUPS])
                which = 0 if part in (SHIFT1, SCALE1) else 1
                if part in (SHIFT1, SHIFT2):
                    link(nc.vector.tensor_tensor(core.shift_cols[:, which], src, bias, ALU.add))
                else:
                    link(nc.vector.tensor_tensor(mcol[:, b], src, bias, ALU.add))
                    link(nc.vector.tensor_scalar(mcol[:, b], mcol[:, b], 1.0, None, ALU.add))
                    gain = gpre[:, which].unsqueeze(2).to_broadcast([P, KB, GROUPS])
                    link(nc.vector.tensor_tensor(core.scale_cols[:, which], mcol[:, b], gain, ALU.mult))

        @block.tensor
        def _(pe):
            pe.wait_ge(wide_done, GROUPS * KB)
            for n, ch in enumerate(order):
                pe.wait_ge(w_in[n % 3], 16 * (n // 3 + 1))
                w = ring[n % 3]
                if ch in gate_chunks:
                    for g in range(GROUPS):
                        r = n * GROUPS + g
                        if r >= 4:
                            pe.wait_ge(rows_read, r - 3)
                        for k in range(KB):
                            last = nc.tensor.matmul(prow[r % 4][:], cwide[:, g, k, :], w[:, k, :],
                                                    start=(k == 0), stop=(k == KB - 1))
                        last.then_inc(rows_done, 1)
                else:
                    for b in range(BPC):
                        j = ch * BPC + b
                        for k in range(KB):
                            last = nc.tensor.matmul(pcol[:, j * GROUPS:(j + 1) * GROUPS], w[:, k, b * P:(b + 1) * P],
                                                    cact[:, k, :], start=(k == 0), stop=(k == KB - 1))
                    last.then_inc(cols_used, 1)


def stage_norm(core, name, source, which):
    nc = core.nc
    BUFS = 3
    with Stage(core, name) as st:
        x = [st.sb(f"x{i}", [P, D]) for i in range(BUFS)]
        sq = st.sb("sq", [P, D])
        ss = st.sb("ss", [P, TILES])
        root = st.sb("root", [P, TILES])
        rstd = st.sb("rstd", [P, TILES])
        pt = [st.psum(f"pt{i}", [P, 4, P]) for i in range(4)]
        x_in = [st.sem(f"x_in{i}") for i in range(BUFS)]
        sq_done = st.sem("sq_done")
        mean_done = st.sem("mean_done")
        root_done = st.sem("root_done")
        recip_done = st.sem("recip_done")
        xn_done = st.sem("xn_done")
        turned = st.sem("turned")
        out_act = st.sem("out_act")
        out_dve = st.sem("out_dve")
        block = st.block()

        @block.sync
        def _(sp):
            for t in range(TILES):
                if t >= BUFS:
                    sp.wait_ge(turned, 2 * (t - BUFS + 1))
                sp.dma_start(x[t % BUFS][:], source[t * P:(t + 1) * P, :]).then_inc(x_in[t % BUFS], 16)

        @block.scalar
        def _(act):
            def evacuate(t):
                act.wait_ge(turned, 2 * t + 1)
                for j in range(4):
                    nc.scalar.activation(core.hT[:, j, t * P:(t + 1) * P], pt[(2 * t) % 4][:, j, :], ACT.Identity,
                                         bias=core.shift_cols[:, which, j, group_of(t):group_of(t) + 1],
                                         scale=core.scale_cols[:, which, j, group_of(t):group_of(t) + 1])\
                        .then_inc(out_act, 1)

            for t in range(TILES):
                act.wait_ge(x_in[t % BUFS], 16 * (t // BUFS + 1))
                if t > 0:
                    act.wait_ge(sq_done, t)
                nc.scalar.activation(sq[:], x[t % BUFS][:], ACT.Square, accum_out=ss[:, t:t + 1]).then_inc(sq_done, 1)
                act.wait_ge(mean_done, t + 1)
                nc.scalar.activation(root[:, t:t + 1], rstd[:, t:t + 1], ACT.Sqrt).then_inc(root_done, 1)
                if t > 0:
                    evacuate(t - 1)
            evacuate(TILES - 1)

        @block.vector
        def _(dve):
            def evacuate(t):
                dve.wait_ge(turned, 2 * t + 2)
                for j in range(4):
                    nc.vector.tensor_scalar(core.hT[:, 4 + j, t * P:(t + 1) * P], pt[(2 * t + 1) % 4][:, j, :],
                                            core.scale_cols[:, which, 4 + j, group_of(t):group_of(t) + 1],
                                            core.shift_cols[:, which, 4 + j, group_of(t):group_of(t) + 1],
                                            ALU.mult, ALU.add).then_inc(out_dve, 1)

            for t in range(TILES):
                r = rstd[:, t:t + 1]
                dve.wait_ge(sq_done, t + 1)
                nc.vector.tensor_scalar(r, ss[:, t:t + 1], 1.0 / D, EPS, ALU.mult, ALU.add).then_inc(mean_done, 1)
                dve.wait_ge(root_done, t + 1)
                nc.vector.reciprocal(r, root[:, t:t + 1]).then_inc(recip_done, 1)
                dve.wait_ge(recip_done, t + 1)
                nc.vector.tensor_scalar(x[t % BUFS][:], x[t % BUFS][:], r, None, ALU.mult).then_inc(xn_done, 1)
                if t > 0:
                    evacuate(t - 1)
            evacuate(TILES - 1)

        @block.tensor
        def _(pe):
            for t in range(TILES):
                pe.wait_ge(xn_done, t + 1)
                if t >= 2:
                    pe.wait_ge(out_act, 4 * (t - 1))
                    pe.wait_ge(out_dve, 4 * (t - 1))
                for half in range(2):
                    for j in range(4):
                        k = 4 * half + j
                        last = nc.tensor.transpose(pt[(2 * t + half) % 4][:, j, :], x[t % BUFS][:, k * P:(k + 1) * P],
                                                   core.ident[:])
                    last.then_inc(turned, 1)


def stage_project(core, out):
    nc, dram = core.nc, core.dram
    CW = 256
    GU, GV, QKV, Z = 0, 512, 1024, 2560
    cols = list(range(GU, 1024, CW)) + list(range(QKV, 3072, CW))
    AB = 2 * UNITS
    RAW = T + 4
    PAD = [0, P + 1, P + 2, T + 3]

    def spans(c):
        a, b = c * TC, (c + 1) * TC
        return [(0, P, 1), (P, b, P + 3)] if c == 0 else [(a, b, a + 3)]

    with Stage(core, "proj") as st:
        w = [st.sb(f"w{i}", [P, KB, CW]) for i in range(2)]
        wab = st.sb("wab", [P, KB, AB])
        raw = [st.sb(f"raw{i}", [P, RAW]) for i in range(2)]
        conv = [st.sb(f"conv{i}", [P, RAW]) for i in range(2)]
        taps = st.sb("taps", [P, 3, 12])
        pf = [st.psum(f"pf{i}", [P, 512]) for i in range(4)]
        pt = [st.psum(f"pt{i}", [P, 4, P]) for i in range(4)]
        small_in = st.sem("small_in")
        w_in = [st.sem(f"w_in{i}") for i in range(2)]
        pads = st.sem("pads")
        made = st.sem("made")
        read = st.sem("read")
        conv_done = st.sem("conv_done")
        silu_done = st.sem("silu_done")
        dve_chain = st.sem("dve_chain")
        turned = st.sem("turned")
        turned_read = st.sem("turned_read")
        block = st.block()

        jobs = []
        for n, at in enumerate(cols):
            if at < GV or QKV <= at < Z:
                for b in range(CW // P):
                    f = (at + b * P - (GU if at < GV else QKV)) // P
                    for c in range(NTC):
                        jobs.append(("gu" if at < GV else "qkv", f, c, n, b))
            else:
                for t in range(TILES):
                    jobs.append(("gv" if at < QKV else "z", t, (at - (GV if at < QKV else Z)) // CW, n, 0))
        for t in range(TILES):
            jobs.append(("ab", t, 0, len(cols), 0))
        qkv_read = {}
        for i, (kind, f, c, n, b) in enumerate(jobs):
            if kind == "qkv" and c == NTC - 1:
                qkv_read[f] = i + 1

        last_job = {n: i for i, (kind, f, c, n, b) in enumerate(jobs)}

        @block.sync
        def _(sp):
            sp.dma_start(taps[:], dram["conv_taps"]).then_inc(small_in, 16)
            sp.dma_start(wab[:], dram["w_in"][:, :, 3072:3072 + AB]).then_inc(small_in, 16)
            for n, at in enumerate(cols):
                if n >= 2:
                    sp.wait_ge(made, last_job[n - 2] + 1)
                sp.dma_start(w[n % 2][:], dram["w_in"][:, :, at:at + CW]).then_inc(w_in[n % 2], 16)

        @block.tensor
        def _(pe):
            def turn(f):
                pe.wait_ge(silu_done, f + 1)
                for q in range(3):
                    r = 3 * f + q
                    if r >= 4:
                        pe.wait_ge(turned_read, r - 3)
                    for t in range(4 * q, min(4 * q + 4, TILES)):
                        at = t * P + (1 if t == 0 else 3)
                        last = nc.tensor.transpose(pt[r % 4][:, t - 4 * q, :], conv[f % 2][:, at:at + P], core.ident[:])
                    last.then_inc(turned, 1)

            seen = -1
            for i, (kind, f, c, n, b) in enumerate(jobs):
                if n != seen:
                    if n < len(cols):
                        pe.wait_ge(w_in[n % 2], 16 * (n // 2 + 1))
                    else:
                        pe.wait_ge(small_in, 2 * 16)
                    seen = n
                if i >= 4:
                    pe.wait_ge(read, i - 3)
                for k in range(KB):
                    if kind in ("gu", "qkv"):
                        dst, lhsT, rhs = pf[i % 4][:, 0:TC], w[n % 2][:, k, b * P:(b + 1) * P], core.hT[:, k, c * TC:(c + 1) * TC]
                    elif kind == "ab":
                        dst, lhsT, rhs = pf[i % 4][:, 0:AB], core.hT[:, k, f * P:(f + 1) * P], wab[:, k, :]
                    else:
                        dst, lhsT, rhs = pf[i % 4][:, 0:CW], core.hT[:, k, f * P:(f + 1) * P], w[n % 2][:, k, :]
                    last = nc.tensor.matmul(dst, lhsT, rhs, start=(k == 0), stop=(k == KB - 1))
                last.then_inc(made, 1)
                if kind == "qkv" and c == NTC - 1 and f >= 1:
                    turn(f - 1)
                if kind == "z" and f == 0 and c == 0:
                    turn(11)

        @block.scalar
        def _(act):
            def silu(f):
                act.wait_ge(conv_done, f + 1)
                nc.scalar.activation(conv[f % 2][:, 1:RAW - 1], conv[f % 2][:, 1:RAW - 1], ACT.Silu).then_inc(silu_done, 1)

            for i, (kind, f, c, n, b) in enumerate(jobs):
                act.wait_ge(made, i + 1)
                src = pf[i % 4]
                if kind == "gu":
                    nc.scalar.activation(out["guT"][:, f, c * TC:(c + 1) * TC], src[:, 0:TC], ACT.Gelu_apprx_tanh).then_inc(read, 1)
                elif kind == "gv":
                    nc.scalar.activation(out["gv"][:, f, c * CW:(c + 1) * CW], src[:, 0:CW], ACT.Gelu_apprx_tanh).then_inc(read, 1)
                elif kind == "z":
                    nc.scalar.activation(out["z"][:, f, c * CW:(c + 1) * CW], src[:, 0:CW], ACT.Silu).then_inc(read, 1)
                elif kind == "ab":
                    nc.scalar.activation(out["ab"][:, f, :], src[:, 0:AB], ACT.Copy).then_inc(read, 1)
                else:
                    if c == 0 and f >= 2:
                        act.wait_ge(conv_done, f - 1)
                    for a, e, at in spans(c):
                        ins = nc.scalar.activation(raw[f % 2][:, at:at + e - a], src[:, a - c * TC:e - c * TC], ACT.Copy)
                    ins.then_inc(read, 1)
                    if c == NTC - 1 and f >= 1:
                        silu(f - 1)
                if kind == "z" and f == 0 and c == 0:
                    silu(11)

        @block.vector
        def _(dve):
            for i in range(2):
                for at in PAD:
                    nc.vector.memset(raw[i][:, at:at + 1], 0.0).then_inc(pads, 1)
            dve.wait_ge(small_in, 2 * 16)
            dve.wait_ge(pads, 2 * len(PAD))
            link = Chain(dve, dve_chain)
            dst = [out["q"], out["k"], out["v"]]

            def convolve(f):
                dve.wait_ge(read, qkv_read[f])
                r, o = raw[f % 2], conv[f % 2]
                if f >= 2:
                    dve.wait_ge(turned, 3 * (f - 1))
                o = o[:, 1:RAW - 1]
                link(nc.vector.tensor_scalar(o, r[:, 0:RAW - 2], taps[:, 0, f:f + 1], None, ALU.mult))
                link(nc.vector.scalar_tensor_tensor(out=o, in0=r[:, 1:RAW - 1], scalar=taps[:, 1, f:f + 1], in1=o,
                                                    op0=ALU.mult, op1=ALU.add))
                nc.vector.scalar_tensor_tensor(out=o, in0=r[:, 2:RAW], scalar=taps[:, 2, f:f + 1], in1=o,
                                               op0=ALU.mult, op1=ALU.add).then_inc(conv_done, 1)

            def place(f):
                for q in range(3):
                    dve.wait_ge(turned, 3 * f + q + 1)
                    n = min(4, TILES - 4 * q)
                    nc.vector.tensor_copy(dst[f // 4][:, 4 * q:4 * q + n, (f % 4) * P:(f % 4 + 1) * P],
                                          pt[(3 * f + q) % 4][:, 0:n, :]).then_inc(turned_read, 1)

            for f in range(12):
                convolve(f)
                if f >= 1:
                    place(f - 1)
            place(11)


def stage_gmlp(core, out):
    nc, dram = core.nc, core.dram
    with Stage(core, "gmlp") as st:
        ws = st.sb("ws", [P, HEADS, P])
        bs = st.sb("bs", [P, HEADS, P])
        sq = [st.sb(f"sq{i}", [P, HEADS, P]) for i in range(2)]
        ss = st.sb("ss", [P, TILES, HEADS])
        rstd = st.sb("rstd", [P, TILES, HEADS])
        tmp = [st.sb(f"tmp{i}", [P, HEADS, P]) for i in range(2)]
        ps = [st.psum(f"ps{i}", [P, HEADS, P]) for i in range(4)]
        small_in = st.sem("small_in")
        squared = st.sem("squared")
        summed = st.sem("summed")
        root_done = st.sem("root_done")
        normed = st.sem("normed")
        mixed = st.sem("mixed")
        mixed_read = st.sem("mixed_read")
        chain = st.sem("chain")
        block = st.block()
        gv, guT = out["gv"], out["guT"]

        @block.sync
        def _(sp):
            sp.dma_start(ws[:], dram["gm_ws"]).then_inc(small_in, 16)
            sp.dma_start(bs[:], dram["gm_bs"].to_broadcast([P, HEADS, P])).then_inc(small_in, 16)

        @block.scalar
        def _(act):
            for t in range(TILES):
                if t >= 2:
                    act.wait_ge(summed, t - 1)
                nc.scalar.activation(sq[t % 2][:], gv[:, t, :].rearrange("p (h d) -> p h d", h=HEADS), ACT.Square)\
                    .then_inc(squared, 1)
            act.wait_ge(summed, TILES + 1)
            nc.scalar.activation(ss[:], rstd[:], ACT.Sqrt).then_inc(root_done, 1)

        @block.vector
        def _(dve):
            link = Chain(dve, chain)
            for t in range(TILES):
                dve.wait_ge(squared, t + 1)
                nc.vector.tensor_reduce(ss[:, t, :], sq[t % 2][:], AX.X, ALU.add).then_inc(summed, 1)
            dve.wait_ge(summed, TILES)
            nc.vector.tensor_scalar(rstd[:], ss[:], 1.0 / P, EPS, ALU.mult, ALU.add).then_inc(summed, 1)
            dve.wait_ge(root_done, 1)
            link(nc.vector.reciprocal(rstd[:], ss[:]))
            for t in range(TILES):
                v = gv[:, t, :].rearrange("p (h d) -> p h d", h=HEADS)
                r = rstd[:, t, :].unsqueeze(2).to_broadcast([P, HEADS, P])
                nc.vector.tensor_tensor(v, v, r, ALU.mult).then_inc(normed, 1)
            dve.wait_ge(small_in, 32)
            for t in range(TILES):
                dve.wait_ge(mixed, t + 1)
                g = guT[:, :, t * P:(t + 1) * P]
                if t >= 2:
                    dve.wait_ge(mixed_read, 2 * (t - 1))
                nc.vector.tensor_tensor(tmp[t % 2][:], ps[t % 4][:], bs[:], ALU.add).then_inc(mixed_read, 1)
                dve.wait_ge(mixed_read, 2 * t + 1)
                nc.vector.tensor_tensor(g, g, tmp[t % 2][:], ALU.mult).then_inc(mixed_read, 1)

        @block.tensor
        def _(pe):
            pe.wait_ge(small_in, 32)
            for t in range(TILES):
                pe.wait_ge(normed, t + 1)
                if t >= 4:
                    pe.wait_ge(mixed_read, 2 * (t - 4) + 1)
                for h in range(HEADS):
                    last = nc.tensor.matmul(ps[t % 4][:, h, :], gv[:, t, h * P:(h + 1) * P], ws[:, h, :], start=True, stop=True)
                last.then_inc(mixed, 1)


def stage_prepare(core, out):
    nc, dram = core.nc, core.dram
    q, k, ab = out["q"], out["k"], out["ab"]
    with Stage(core, "prep") as st:
        rope_c = st.sb("rope_c", [P, TILES - 1, P])
        rope_s = st.sb("rope_s", [P, TILES - 1, P])
        par = st.sb("par", [P, 2, UNITS])
        work = st.sb("work", [P, HW])
        work2 = st.sb("work2", [P, HW])
        ss = st.sb("ss", [P, TILES, 2, HEADS])
        rt = st.sb("rt", [P, TILES, 2, HEADS])
        x = st.sb("x", [P, TILES, UNITS])
        neg = st.sb("neg", [P, TILES, UNITS])
        low = st.sb("low", [P, TILES, UNITS])
        g = out["g"]
        beta = out["beta"]
        pg = st.psum("pg", [P, 512])
        pt = [st.psum(f"pt{i}", [P, 4, P]) for i in range(4)]
        small_in = st.sem("small_in")
        ch = st.sem("chain")
        to_act = st.sem("to_act")
        from_act = st.sem("from_act")
        qk_done = st.sem("qk_done")
        turned = st.sem("turned")
        turned_read = st.sem("turned_read")
        sums_done = st.sem("sums_done")
        rest_done = st.sem("rest_done")
        block = st.block()

        @block.sync
        def _(sp):
            sp.dma_start(rope_c[:], dram["rope_cos"]).then_inc(small_in, 16)
            sp.dma_start(rope_s[:], dram["rope_sin"]).then_inc(small_in, 16)
            sp.dma_start(par[:], dram["decay_rows"].to_broadcast([P, 2, UNITS])).then_inc(small_in, 16)

        @block.vector
        def _(dve):
            link = Chain(dve, ch)
            dve.wait_ge(small_in, 48)
            a = ab[:, :, 0:UNITS]
            b = ab[:, :, UNITS:2 * UNITS]
            dt = par[:, 1, :].unsqueeze(1).to_broadcast([P, TILES, UNITS])
            link(nc.vector.tensor_tensor(x[:], a, dt, ALU.add))
            link(nc.vector.tensor_scalar(neg[:], x[:], -1.0, None, ALU.mult))
            link(nc.vector.tensor_tensor(low[:], x[:], neg[:], ALU.min))
            nc.vector.tensor_scalar(x[:], x[:], 0.0, None, ALU.max).then_inc(to_act, 1)
            for t in range(TILES):
                for j, src in enumerate((q, k)):
                    link(nc.vector.tensor_tensor(work[:], src[:, t, :], src[:, t, :], ALU.mult))
                    link(nc.vector.tensor_reduce(ss[:, t, j, :], work[:].rearrange("p (h d) -> p h d", h=HEADS), AX.X, ALU.add))
            nc.vector.tensor_scalar(ss[:], ss[:], EPS, None, ALU.add).then_inc(to_act, 1)
            dve.wait_ge(from_act, 4)
            link(nc.vector.tensor_scalar(beta[:], beta[:], 1.0, None, ALU.add))
            link(nc.vector.reciprocal(beta[:], beta[:]))
            link(nc.vector.tensor_tensor(x[:], x[:], low[:], ALU.add))
            rate = par[:, 0, :].unsqueeze(1).to_broadcast([P, TILES, UNITS])
            link(nc.vector.tensor_tensor(x[:], x[:], rate, ALU.mult))
            nc.vector.tensor_scalar(g[:], x[:], -1.0, None, ALU.mult).then_inc(to_act, 1)
            dve.wait_ge(from_act, 5)
            link(nc.vector.reciprocal(ss[:], rt[:]))
            link(nc.vector.tensor_scalar(ss[:, :, 0, :], ss[:, :, 0, :], float(P) ** -0.5, None, ALU.mult))
            for t in range(TILES):
                for j, src in enumerate((q, k)):
                    heads = src[:, t, :].rearrange("p (h d) -> p h d", h=HEADS)
                    r = ss[:, t, j, :].unsqueeze(2).to_broadcast([P, HEADS, P])
                    if t == 0:
                        nc.vector.tensor_tensor(heads, heads, r, ALU.mult).then_inc(qk_done, 1)
                        continue
                    link(nc.vector.tensor_tensor(heads, heads, r, ALU.mult))
                    cos = rope_c[:, t - 1, :].unsqueeze(1).to_broadcast([P, HEADS, P])
                    w3 = work[:].rearrange("p (h d) -> p h d", h=HEADS)
                    nc.vector.tensor_tensor(w3, heads, cos, ALU.mult).then_inc(ch, 1)
                    link.n += 1
                    s4 = src[:, t, :].rearrange("p (h e d) -> p h e d", h=2 * HEADS, e=2)
                    w4 = work2[:].rearrange("p (h e d) -> p h e d", h=2 * HEADS, e=2)
                    for e in range(2):
                        for half in range(2):
                            sin = rope_s[:, t - 1, half * 64 + e * 32:half * 64 + e * 32 + 32]
                            ins = nc.vector.tensor_tensor(w4[:, half::2, e, :], s4[:, half::2, 1 - e, :],
                                                          sin.unsqueeze(1).to_broadcast([P, HEADS, 32]), ALU.mult)
                            ins.then_inc(ch, 1)
                            link.n += 1
                    dve.wait_ge(ch, link.n)
                    nc.vector.tensor_tensor(src[:, t, :], work[:], work2[:], ALU.add).then_inc(qk_done, 1)
                    dve.wait_ge(qk_done, 2 * t + j + 1)

        @block.scalar
        def _(act):
            act.wait_ge(small_in, 48)
            act.wait_ge(to_act, 1)
            nc.scalar.activation(low[:], low[:], ACT.Exp).then_inc(from_act, 1)
            nc.scalar.activation(par[:, 0, :], par[:, 0, :], ACT.Exp).then_inc(from_act, 1)
            nc.scalar.activation(beta[:], ab[:, :, UNITS:2 * UNITS], ACT.Exp, scale=-1.0).then_inc(from_act, 1)
            act.wait_ge(from_act, 1)
            nc.scalar.activation(low[:], low[:], ACT.Ln, bias=1.0).then_inc(from_act, 1)
            act.wait_ge(to_act, 2)
            nc.scalar.activation(rt[:], ss[:], ACT.Sqrt).then_inc(from_act, 1)
            act.wait_ge(sums_done, 1)
            cum = pg[:, 0:TILES * UNITS].rearrange("p (t u) -> p t u", t=TILES)
            tot = pg[:, 128:128 + TILES * UNITS].rearrange("p (t u) -> p t u", t=TILES)
            nc.scalar.activation(out["neg_cum"][:], cum, ACT.Copy, scale=-1.0).then_inc(from_act, 1)
            nc.scalar.activation(out["exp_cum"][:], cum, ACT.Exp)
            nc.scalar.activation(out["exp_tot"][:], tot, ACT.Exp)
            act.wait_ge(from_act, 6)
            nc.scalar.activation(x[:], tot, ACT.Copy).then_inc(from_act, 1)
            act.wait_ge(rest_done, 1)
            nc.scalar.activation(out["exp_rest"][:], out["exp_rest"][:], ACT.Exp)
            for i in range(2 * TILES):
                act.wait_ge(turned, i + 1)
                nc.scalar.activation(core.hT[:, 4 * (i % 2):4 * (i % 2) + 4, (i // 2) * P:(i // 2 + 1) * P], pt[i % 4][:],
                                     ACT.Copy).then_inc(turned_read, 1)

        @block.gpsimd
        def _(pool):
            pool.wait_ge(from_act, 7)
            nc.gpsimd.tensor_tensor(out["exp_rest"][:], x[:], out["neg_cum"][:], ALU.add).then_inc(rest_done, 1)

        @block.tensor
        def _(pe):
            pe.wait_ge(to_act, 3)
            for d in range(2):
                for src_m, base in ((core.tri[:, d, :], 0), (core.ones[:], 128)):
                    dst = pg[:, base:base + TILES * UNITS].rearrange("p (t u) -> p t u", t=TILES)[:, :, 4 * d:4 * d + 4]
                    last = nc.tensor.matmul(dst, src_m, g[:, :, 4 * d:4 * d + 4], start=True, stop=True)
            last.then_inc(sums_done, 1)
            for i in range(2 * TILES):
                t, src = i // 2, (q, k)[i % 2]
                pe.wait_ge(qk_done, i + 1)
                if i >= 4:
                    pe.wait_ge(turned_read, i - 3)
                for h in range(HEADS):
                    last = nc.tensor.transpose(pt[i % 4][:, h, :], src[:, t, h * P:(h + 1) * P], core.ident[:])
                last.then_inc(turned, 1)


def stage_scan(core, out):
    nc, dram = core.nc, core.dram
    qT, kT = core.hT[:, 0:4, :], core.hT[:, 4:8, :]
    k, v, g, beta, o = out["k"], out["v"], out["g"], out["beta"], out["q"]
    tiles = [list(range(TILES)), [0] + list(range(TILES - 1, 0, -1))]
    S4 = [P, HEADS, P]
    NPE, NDVE, NACT, NPOOL = 17, 20, 8, 10

    pe_products = lambda n: NPE * n + 1
    pe_join = lambda n, l: NPE * n + (2 if l == 0 else 1 + 2 * l)
    pe_double = lambda n, l: NPE * n + 2 + 2 * l
    pe_w = lambda n: NPE * n + 15
    pe_u = lambda n: NPE * n + 16
    pe_o = lambda n: NPE * n + 17
    act_decay = lambda n: NACT * n + 1
    act_join = lambda n, l: NACT * n + 1 + l
    act_w = lambda n: NACT * n + 8
    dve_attn = lambda n: NDVE * n + 1
    dve_b = lambda n: NDVE * n + 2
    dve_r = lambda n, l: NDVE * n + 3 + 2 * l
    dve_v = lambda n, l: NDVE * n + 4 + 2 * l
    dve_new = lambda n: NDVE * n + 16
    dve_o1 = lambda n: NDVE * n + 17
    dve_s1 = lambda n: NDVE * n + 18
    dve_s2 = lambda n: NDVE * n + 19
    dve_o2 = lambda n: NDVE * n + 20
    pool_mask = lambda n, l: NPOOL * n + (1, 2, 4, 6, 7, 8, 9)[l]
    pool_ek = lambda n: NPOOL * n + 3
    pool_kd = lambda n: NPOOL * n + 5
    pool_o = lambda n: NPOOL * n + 10

    with Stage(core, "scan") as st:
        both = lambda name: [st.sb(f"{name}{s}", S4) for s in range(2)]
        level = st.sb("level", [P, 2, LEVELS, P])
        far = st.sb("far", [P, 2, P])
        D, B, R, V, Z = both("D"), both("B"), both("R"), both("V"), both("Z")
        M = [[st.sb(f"M{s}{i}", S4) for i in range(2)] for s in range(2)]
        attn, ek, kd, new = both("attn"), both("ek"), both("kd"), both("new")
        nW = Z
        osum = D
        S = [[st.sb(f"S{s}{i}", S4) for i in range(2)] for s in range(2)]
        bank = [[st.psum(f"b{s}{i}", S4) for i in range(4)] for s in range(2)]
        small_in = st.sem("small_in")
        cleared = st.sem("cleared")
        states_out = st.sem("states_out")
        pe_s = [st.sem(f"pe{s}") for s in range(2)]
        act_s = [st.sem(f"act{s}") for s in range(2)]
        dve_s = [st.sem(f"dve{s}") for s in range(2)]
        pool_s = [st.sem(f"pool{s}") for s in range(2)]
        block = st.block()

        def wide(col):
            return col.unsqueeze(2).to_broadcast(S4)

        def at(x, s, c):
            return x[:, c, 4 * s:4 * s + 4]

        def heads(x, c):
            return x[:, c, :].rearrange("p (h d) -> p h d", h=HEADS)

        ident4 = core.ident[:].unsqueeze(1).to_broadcast(S4)

        @block.sync
        def _(sp):
            sp.dma_start(level[:], dram["level_masks"]).then_inc(small_in, 16)
            sp.dma_start(far[:], dram["far_masks"]).then_inc(small_in, 16)
            for s in range(2):
                sp.dma_start(S[s][1][:], dram["state"][s]).then_inc(small_in, 16)
            for s in range(2):
                sp.wait_ge(dve_s[s], dve_s2(0))
                sp.dma_start(dram["new_state"][s], S[s][0][:]).then_inc(states_out, 16)
            sp.wait_ge(states_out, 32)

        @block.gpsimd
        def _(pool):
            nc.gpsimd.memset(o[:], 0.0).then_inc(cleared, 1)
            for s in range(2):
                nc.gpsimd.memset(S[s][0][:], 0.0).then_inc(cleared, 1)
            pool.wait_ge(cleared, 3)
            pool.wait_ge(small_in, 64)
            for n in range(TILES):
                for l in range(LEVELS):
                    for s in range(2):
                        c = tiles[s][n]
                        if l == 0:
                            pool.wait_ge(dve_s[s], dve_b(n))
                            if n > 0:
                                pool.wait_ge(pe_s[s], pe_join(n - 1, LEVELS - 1))
                        elif l >= 2:
                            pool.wait_ge(pe_s[s], pe_join(n, l - 2))
                            if l == 2:
                                pool.wait_ge(dve_s[s], dve_r(n, 0))
                        elif n > 0:
                            pool.wait_ge(pe_s[s], pe_join(n - 1, LEVELS - 2))
                        m = level[:, s, l, :].unsqueeze(1).to_broadcast(S4)
                        nc.gpsimd.tensor_tensor(M[s][l % 2][:], B[s][:], m, ALU.mult).then_inc(pool_s[s], 1)
                        if l == 1:
                            if n > 0:
                                pool.wait_ge(pe_s[s], pe_w(n - 1))
                            nc.gpsimd.tensor_tensor(ek[s][:], heads(k, c), wide(at(out["exp_cum"], s, c)), ALU.mult)\
                                .then_inc(pool_s[s], 1)
                        if l == 2:
                            if n > 0:
                                pool.wait_ge(pe_s[s], pe_o(n - 1))
                            nc.gpsimd.tensor_tensor(kd[s][:], heads(k, c), wide(at(out["exp_rest"], s, c)), ALU.mult)\
                                .then_inc(pool_s[s], 1)
                for s in range(2):
                    c = tiles[s][n]
                    pool.wait_ge(dve_s[s], dve_o2(n))
                    if s == 1:
                        pool.wait_ge(pool_s[0], pool_o(n))
                    elif n > 0:
                        pool.wait_ge(pool_s[1], pool_o(n - 1))
                    nc.gpsimd.tensor_tensor(heads(o, c), heads(o, c), osum[s][:], ALU.add).then_inc(pool_s[s], 1)

        @block.scalar
        def _(act):
            for n in range(TILES):
                for s in range(2):
                    c = tiles[s][n]
                    act.wait_ge(pe_s[s], pe_products(n))
                    if n > 0:
                        act.wait_ge(pool_s[s], pool_o(n - 1))
                    for h in range(HEADS):
                        ins = nc.scalar.activation(D[s][:, h, :], bank[s][2][:, h, :], ACT.Exp,
                                                   bias=out["neg_cum"][:, c, 4 * s + h:4 * s + h + 1])
                    ins.then_inc(act_s[s], 1)
                for l in range(1, LEVELS):
                    for s in range(2):
                        act.wait_ge(pe_s[s], pe_join(n, l))
                        nc.scalar.activation(Z[s][:], bank[s][0][:], ACT.Copy).then_inc(act_s[s], 1)
                for s in range(2):
                    act.wait_ge(pe_s[s], pe_w(n))
                    nc.scalar.activation(nW[s][:], bank[s][0][:], ACT.Copy, scale=-1.0).then_inc(act_s[s], 1)

        @block.vector
        def _(dve):
            for n in range(TILES):
                for s in range(2):
                    c = tiles[s][n]
                    dve.wait_ge(act_s[s], act_decay(n))
                    nc.vector.tensor_tensor(attn[s][:], bank[s][1][:], D[s][:], ALU.mult).then_inc(dve_s[s], 1)
                    for h in range(HEADS):
                        ins = nc.vector.scalar_tensor_tensor(out=B[s][:, h, :], in0=bank[s][0][:, h, :],
                                                             scalar=beta[:, c, 4 * s + h:4 * s + h + 1], in1=D[s][:, h, :],
                                                             op0=ALU.mult, op1=ALU.mult)
                    ins.then_inc(dve_s[s], 1)
                for s in range(2):
                    dve.wait_ge(pool_s[s], pool_mask(n, 0))
                    nc.vector.tensor_tensor(R[s][:], ident4, M[s][0][:], ALU.subtract).then_inc(dve_s[s], 1)
                    dve.wait_ge(pe_s[s], pe_join(n, 0))
                    nc.vector.tensor_tensor(V[s][:], ident4, bank[s][0][:], ALU.subtract).then_inc(dve_s[s], 1)
                for l in range(1, LEVELS):
                    for s in range(2):
                        dve.wait_ge(pe_s[s], pe_double(n, l))
                        dve.wait_ge(dve_s[s], dve_r(n, l - 1))
                        nc.vector.tensor_tensor(R[s][:], R[s][:], bank[s][2][:], ALU.subtract).then_inc(dve_s[s], 1)
                        if l < LEVELS - 1:
                            dve.wait_ge(dve_s[s], dve_v(n, l - 1))
                            nc.vector.tensor_tensor(V[s][:], V[s][:], bank[s][1][:], ALU.subtract).then_inc(dve_s[s], 1)
                for s in range(2):
                    c = tiles[s][n]
                    dve.wait_ge(pe_s[s], pe_u(n))
                    nc.vector.tensor_tensor(new[s][:], bank[s][1][:], wide(at(beta, s, c)), ALU.mult).then_inc(dve_s[s], 1)
                for s in range(2):
                    c = tiles[s][n]
                    state = S[s][0 if n == 0 else 1]
                    dve.wait_ge(pe_s[s], pe_o(n))
                    nc.vector.tensor_tensor(osum[s][:], bank[s][2][:], wide(at(out["exp_cum"], s, c)), ALU.mult)\
                        .then_inc(dve_s[s], 1)
                    nc.vector.tensor_tensor(state[:], state[:], wide(at(out["exp_tot"], s, c)), ALU.mult)\
                        .then_inc(dve_s[s], 1)
                    dve.wait_ge(dve_s[s], dve_s1(n))
                    nc.vector.tensor_tensor(state[:], state[:], bank[s][0][:], ALU.add).then_inc(dve_s[s], 1)
                    nc.vector.tensor_tensor(osum[s][:], osum[s][:], bank[s][3][:], ALU.add).then_inc(dve_s[s], 1)

        @block.tensor
        def _(pe):
            mm = nc.tensor.matmul
            pe.wait_ge(small_in, 64)
            pe.wait_ge(cleared, 3)
            for n in range(TILES):
                for s in range(2):
                    c = tiles[s][n]
                    t = slice(c * P, (c + 1) * P)
                    b = bank[s]
                    if n > 0:
                        pe.wait_ge(dve_s[s], dve_o2(n - 1))
                    for h in range(HEADS):
                        mm(b[0][:, h, :], kT[:, h, t], kT[:, h, t], start=True, stop=True)
                    for h in range(HEADS):
                        mm(b[1][:, h, :], kT[:, h, t], qT[:, h, t], start=True, stop=True)
                    mm(b[2][:], core.ident[:], far[:, s, :].unsqueeze(1).to_broadcast(S4), start=True, stop=False)
                    for h in range(HEADS):
                        gcol = g[:, c, 4 * s + h:4 * s + h + 1].to_broadcast([P, P])
                        last = mm(b[2][:, h, :], gcol, core.tri[:, s, :], start=False, stop=(h == HEADS - 1))
                    last.then_inc(pe_s[s], 1)
                for s in range(2):
                    pe.wait_ge(pool_s[s], pool_mask(n, 0))
                    for h in range(HEADS):
                        last = mm(bank[s][0][:, h, :], M[s][0][:, h, :], core.ident[:], start=True, stop=True)
                    last.then_inc(pe_s[s], 1)
                for l in range(1, LEVELS):
                    for s in range(2):
                        pe.wait_ge(pool_s[s], pool_mask(n, l))
                        pe.wait_ge(dve_s[s], dve_v(n, l - 1))
                        for h in range(HEADS):
                            last = mm(bank[s][0][:, h, :], M[s][l % 2][:, h, :], V[s][:, h, :], start=True, stop=True)
                        last.then_inc(pe_s[s], 1)
                    for s in range(2):
                        pe.wait_ge(act_s[s], act_join(n, l))
                        for h in range(HEADS):
                            last = mm(bank[s][2][:, h, :], Z[s][:, h, :], R[s][:, h, :], start=True, stop=True)
                        if l < LEVELS - 1:
                            for h in range(HEADS):
                                last = mm(bank[s][1][:, h, :], R[s][:, h, :], Z[s][:, h, :], start=True, stop=True)
                        last.then_inc(pe_s[s], 1)
                for s in range(2):
                    pe.wait_ge(dve_s[s], dve_r(n, LEVELS - 1))
                    pe.wait_ge(pool_s[s], pool_ek(n))
                    for h in range(HEADS):
                        last = mm(bank[s][0][:, h, :], ek[s][:, h, :], R[s][:, h, :], start=True, stop=True)
                    last.then_inc(pe_s[s], 1)
                for s in range(2):
                    state = S[s][0 if n == 0 else 1]
                    pe.wait_ge(act_s[s], act_w(n))
                    for h in range(HEADS):
                        mm(bank[s][1][:, h, :], R[s][:, h, :], v[:, tiles[s][n], h * P:(h + 1) * P], start=True, stop=False)
                        last = mm(bank[s][1][:, h, :], nW[s][:, h, :], state[:, h, :], start=False, stop=True)
                    last.then_inc(pe_s[s], 1)
                for s in range(2):
                    c = tiles[s][n]
                    t = slice(c * P, (c + 1) * P)
                    state = S[s][0 if n == 0 else 1]
                    for h in range(HEADS):
                        mm(bank[s][2][:, h, :], qT[:, h, t], state[:, h, :], start=True, stop=True)
                    pe.wait_ge(dve_s[s], dve_new(n))
                    pe.wait_ge(pool_s[s], pool_kd(n))
                    for h in range(HEADS):
                        mm(bank[s][3][:, h, :], attn[s][:, h, :], new[s][:, h, :], start=True, stop=True)
                    for h in range(HEADS):
                        last = mm(bank[s][0][:, h, :], kd[s][:, h, :], new[s][:, h, :], start=True, stop=True)
                    last.then_inc(pe_s[s], 1)


def stage_out(core, out):
    nc, dram = core.nc, core.dram
    o, z, oaT, obT = out["q"], out["z"], out["guT"], core.hT[:, 0:HEADS, :]
    with Stage(core, "out") as st:
        wo = st.sb("wo", [P, KB, D])
        nrow = st.sb("nrow", [P, P])
        gate = st.sb("gate", [P, GROUPS, D])
        sq = [st.sb(f"sq{i}", [P, HW]) for i in range(2)]
        ss = st.sb("ss", [P, TILES, HEADS])
        rstd = st.sb("rstd", [P, TILES, HEADS])
        x = [st.sb(f"x{i}", [P, D]) for i in range(2)]
        y = [st.sb(f"y{i}", [P, D]) for i in range(2)]
        ysq = st.sb("ysq", [P, D])
        ys = st.sb("ys", [P, TILES])
        yr = st.sb("yr", [P, TILES])
        pt = [st.psum(f"pt{i}", [P, HEADS, P]) for i in range(2)]
        py = [st.psum(f"py{i}", [P, 2, HW]) for i in range(2)]
        small_in = st.sem("small_in")
        x_in = [st.sem(f"x_in{i}") for i in range(2)]
        x_out = [st.sem(f"x_out{i}") for i in range(2)]
        squared = st.sem("squared")
        summed = st.sem("summed")
        root_done = st.sem("root_done")
        o_chain = st.sem("o_chain")
        gated = st.sem("gated")
        turned = st.sem("turned")
        turned_read = st.sem("turned_read")
        y_done = st.sem("y_done")
        y_sq = st.sem("y_sq")
        y_root = st.sem("y_root")
        y_mean = st.sem("y_mean")
        y_chain = st.sem("y_chain")
        x1_done = st.sem("x1_done")
        block = st.block()

        @block.sync
        def _(sp):
            sp.dma_start(nrow[:], dram["norm_row"].to_broadcast([P, P])).then_inc(small_in, 16)
            sp.dma_start(gate[:], dram["gate_rows"][0]).then_inc(small_in, 16)
            sp.dma_start(wo[:], dram["w_out"]).then_inc(small_in, 16)
            for t in range(TILES):
                if t >= 2:
                    sp.wait_ge(x1_done, t - 1)
                sp.dma_start(x[t % 2][:], dram["x"][t * P:(t + 1) * P, :]).then_inc(x_in[t % 2], 16)

        @block.gpsimd
        def _(pool):
            for t in range(TILES):
                pool.wait_ge(x1_done, t + 1)
                pool.dma_start(dram["x1"][t * P:(t + 1) * P, :], y[t % 2][:]).then_inc(x_out[t % 2], 16)
            for i in range(2):
                pool.wait_ge(x_out[i], 16 * ((TILES + 1 - i) // 2))

        @block.scalar
        def _(act):
            def rms(t):
                act.wait_ge(y_done, t + 1)
                if t > 0:
                    act.wait_ge(y_sq, t)
                nc.scalar.activation(ysq[:], py[t % 2][:].rearrange("p a b -> p (a b)"), ACT.Square,
                                     accum_out=ys[:, t:t + 1]).then_inc(y_sq, 1)
                act.wait_ge(y_mean, t + 1)
                nc.scalar.activation(ys[:, t:t + 1], yr[:, t:t + 1], ACT.Sqrt).then_inc(y_root, 1)

            for t in range(TILES):
                if t >= 2:
                    act.wait_ge(summed, t - 1)
                nc.scalar.activation(sq[t % 2][:], o[:, t, :], ACT.Square).then_inc(squared, 1)
            act.wait_ge(summed, TILES + 1)
            nc.scalar.activation(ss[:], rstd[:], ACT.Sqrt).then_inc(root_done, 1)
            for t in range(TILES):
                act.wait_ge(turned, t + 1)
                nc.scalar.activation(obT[:, :, t * P:(t + 1) * P], pt[t % 2][:], ACT.Copy).then_inc(turned_read, 1)
                if t > 0:
                    rms(t - 1)
            rms(TILES - 1)

        @block.vector
        def _(dve):
            for t in range(TILES):
                dve.wait_ge(squared, t + 1)
                nc.vector.tensor_reduce(ss[:, t, :], sq[t % 2][:].rearrange("p (h d) -> p h d", h=HEADS), AX.X,
                                        ALU.add).then_inc(summed, 1)
            dve.wait_ge(summed, TILES)
            nc.vector.tensor_scalar(rstd[:], ss[:], 1.0 / P, EPS, ALU.mult, ALU.add).then_inc(summed, 1)
            dve.wait_ge(root_done, 1)
            link = Chain(dve, o_chain)
            link(nc.vector.reciprocal(rstd[:], ss[:]))
            dve.wait_ge(small_in, 48)
            for t in range(TILES):
                zt = z[:, t, :].rearrange("p (h d) -> p h d", h=HEADS)
                ot = o[:, t, :].rearrange("p (h d) -> p h d", h=HEADS)
                link(nc.vector.tensor_tensor(zt, zt, nrow[:].unsqueeze(1).to_broadcast([P, HEADS, P]), ALU.mult))
                link(nc.vector.tensor_tensor(ot, ot, rstd[:, t, :].unsqueeze(2).to_broadcast([P, HEADS, P]), ALU.mult))
                nc.vector.tensor_tensor(ot, ot, zt, ALU.mult).then_inc(gated, 1)
            link = Chain(dve, y_chain)
            for t in range(TILES):
                r = yr[:, t:t + 1]
                dve.wait_ge(y_sq, t + 1)
                nc.vector.tensor_scalar(r, ys[:, t:t + 1], 1.0 / D, EPS, ALU.mult, ALU.add).then_inc(y_mean, 1)
                dve.wait_ge(y_root, t + 1)
                link(nc.vector.reciprocal(r, ys[:, t:t + 1]))
                if t >= 2:
                    dve.wait_ge(x_out[t % 2], 16 * (t // 2))
                link(nc.vector.scalar_tensor_tensor(out=y[t % 2][:], in0=py[t % 2][:].rearrange("p a b -> p (a b)"), scalar=r,
                                                    in1=gate[:, group_of(t), :], op0=ALU.mult, op1=ALU.mult))
                dve.wait_ge(x_in[t % 2], 16 * (t // 2 + 1))
                nc.vector.tensor_tensor(y[t % 2][:], y[t % 2][:], x[t % 2][:], ALU.add).then_inc(x1_done, 1)

        @block.tensor
        def _(pe):
            def project(t):
                pe.wait_ge(turned_read, t + 1)
                if t == 0:
                    pe.wait_ge(small_in, 48)
                if t >= 2:
                    pe.wait_ge(x1_done, t - 1)
                for half in range(2):
                    for k in range(KB):
                        src = oaT[:, k, t * P:(t + 1) * P] if k < HEADS else obT[:, k - HEADS, t * P:(t + 1) * P]
                        last = nc.tensor.matmul(py[t % 2][:, half, :], src, wo[:, k, half * HW:(half + 1) * HW],
                                                start=(k == 0), stop=(k == KB - 1))
                last.then_inc(y_done, 1)

            for t in range(TILES):
                pe.wait_ge(gated, t + 1)
                if t >= 2:
                    pe.wait_ge(turned_read, t - 1)
                for h in range(HEADS):
                    last = nc.tensor.transpose(pt[t % 2][:, h, :], o[:, t, h * P:(h + 1) * P], core.ident[:])
                last.then_inc(turned, 1)
                if t > 0:
                    project(t - 1)
            project(TILES - 1)


def stage_queries(core, hT):
    nc, dram = core.nc, core.dram
    HP = 2 * PH
    GH = 4
    CW = GH * P
    with Stage(core, "query") as st:
        w = [st.sb(f"w{i}", [P, KB, CW // 2]) for i in range(2)]
        keys = st.sb("keys", [P, HP, P])
        q = st.sb("q", [P, GH, T])
        s = [st.sb(f"s{i}", [P, CW]) for i in range(2)]
        pq = [st.psum(f"pq{i}", [P, 512]) for i in range(4)]
        ps = [st.psum(f"ps{i}", [P, CW]) for i in range(4)]
        keys_in = st.sem("keys_in")
        w_in = [st.sem(f"w_in{i}") for i in range(2)]
        q_made = st.sem("q_made")
        q_read = st.sem("q_read")
        s_made = st.sem("s_made")
        s_read = st.sem("s_read")
        s_out = [st.sem(f"s_out{i}") for i in range(2)]
        h_out = st.sem("h_out")
        block = st.block()
        GR = HP // GH
        PERG = GH * NTC

        @block.sync
        def _(sp):
            sp.dma_start(keys[:], dram["peer_keys"]).then_inc(keys_in, 16)
            for n in range(2 * GR):
                if n >= 2:
                    sp.wait_ge(q_made, PERG // 2 * (n - 1))
                sp.dma_start(w[n % 2][:], dram["peer_wq"][:, :, n * CW // 2:(n + 1) * CW // 2]).then_inc(w_in[n % 2], 16)

        @block.gpsimd
        def _(pool):
            pool.dma_start(dram["h2T"], hT[:]).then_inc(h_out, 16)
            i = 0
            for g in range(GR):
                for t in range(TILES):
                    pool.wait_ge(s_read, i + 1)
                    pool.dma_start(dram["scores"][t * P:(t + 1) * P, g * CW:(g + 1) * CW], s[i % 2][:]).then_inc(s_out[i % 2], 16)
                    i += 1
            for j in range(2):
                pool.wait_ge(s_out[j], 16 * (GR * TILES // 2))
            pool.wait_ge(h_out, 16)

        @block.scalar
        def _(act):
            i = 0
            for g in range(GR):
                if g > 0:
                    act.wait_ge(s_made, TILES * g)
                for b in range(GH):
                    for c in range(NTC):
                        act.wait_ge(q_made, i + 1)
                        nc.scalar.activation(q[:, b, c * TC:(c + 1) * TC], pq[i % 4][:, 0:TC], ACT.Copy).then_inc(q_read, 1)
                        i += 1

        @block.vector
        def _(dve):
            for i in range(GR * TILES):
                dve.wait_ge(s_made, i + 1)
                if i >= 2:
                    dve.wait_ge(s_out[i % 2], 16 * (i // 2))
                nc.vector.tensor_copy(s[i % 2][:], ps[i % 4][:]).then_inc(s_read, 1)

        @block.tensor
        def _(pe):
            i = 0
            pe.wait_ge(keys_in, 16)
            for g in range(GR):
                for b in range(GH):
                    n = 2 * g + b // 2
                    pe.wait_ge(w_in[n % 2], 16 * (n // 2 + 1))
                    for c in range(NTC):
                        if i >= 4:
                            pe.wait_ge(q_read, i - 3)
                        for k in range(KB):
                            last = nc.tensor.matmul(pq[i % 4][:, 0:TC], w[n % 2][:, k, (b % 2) * P:(b % 2 + 1) * P],
                                                    hT[:, k, c * TC:(c + 1) * TC], start=(k == 0), stop=(k == KB - 1))
                        last.then_inc(q_made, 1)
                        i += 1
                pe.wait_ge(q_read, i)
                for t in range(TILES):
                    j = g * TILES + t
                    if j >= 4:
                        pe.wait_ge(s_read, j - 3)
                    for b in range(GH):
                        last = nc.tensor.matmul(ps[j % 4][:, b * P:(b + 1) * P], q[:, b, t * P:(t + 1) * P],
                                                keys[:, g * GH + b, :], start=True, stop=True)
                    last.then_inc(s_made, 1)


def stage_topk(core):
    nc, dram = core.nc, core.dram
    K = TOPK
    HP = 2 * PH
    with Stage(core, "topk") as st:
        s = [st.sb(f"s{i}", [P, HP, P]) for i in range(2)]
        rest = st.sb("rest", [P, HP, P])
        sv = st.sb("sv", [P, PH, 2, K])
        si = st.sb("si", [P, PH, 2, K], U32)
        sif = st.sb("sif", [P, PH, 2, K])
        cand = st.sb("cand", [P, PH, K, K])
        crest = st.sb("crest", [P, PH, K, K])
        cv = st.sb("cv", [P, PH, K])
        ci = st.sb("ci", [P, PH, K], U32)
        part = st.sb("part", [P, 2, PH, K], U32)
        partf = st.sb("partf", [P, 2, PH, K])
        pick = st.sb("pick", [P, SLOTS, K])
        gate = [st.sb(f"gate{i}", [P, PH, K]) for i in range(2)]
        num = [st.sb(f"num{i}", [P, 2, SLOTS]) for i in range(2)]
        zsum = st.sb("zsum", [P, PH])
        iota = st.sb("iota", [P, K])
        pt = [st.psum(f"pt{i}", [P, 3, P]) for i in range(2)]
        s_in = [st.sem(f"s_in{i}") for i in range(2)]
        iota_done = st.sem("iota_done")
        scores_used = st.sem("scores_used")
        ch = st.sem("chain")
        exp_in = st.sem("exp_in")
        exp_done = st.sem("exp_done")
        tile_done = st.sem("tile_done")
        turned = st.sem("turned")
        turned_read = st.sem("turned_read")
        block = st.block()

        @block.sync
        def _(sp):
            for t in range(TILES):
                if t >= 2:
                    sp.wait_ge(scores_used, t - 1)
                sp.dma_start(s[t % 2][:], dram["scores"][t * P:(t + 1) * P, :].rearrange("t (h n) -> t h n", n=P))\
                    .then_inc(s_in[t % 2], 16)

        @block.gpsimd
        def _(pool):
            nc.gpsimd.iota(iota[:], [[1, K]], base=0, channel_multiplier=0, allow_small_or_imprecise_dtypes=True)\
                .then_inc(iota_done, 1)

        @block.vector
        def _(dve):
            link = Chain(dve, ch)
            v = nc.vector

            def step(ins):
                link.n += 1
                ins.then_inc(ch, 1)

            dve.wait_ge(iota_done, 1)
            for t in range(TILES):
                x = s[t % 2]
                dve.wait_ge(s_in[t % 2], 16 * (t // 2 + 1))
                for j in range(HP):
                    step(v.max(sv[:, j // 2, j % 2, 0:8], x[:, j, :]))
                for j in range(HP):
                    if j == 0:
                        dve.wait_ge(ch, link.n)
                    step(v.max_index(si[:, j // 2, j % 2, 0:8], sv[:, j // 2, j % 2, 0:8], x[:, j, :]))
                    step(v.match_replace(rest[:, j, :], sv[:, j // 2, j % 2, 0:8], x[:, j, :], LOWEST))
                dve.wait_ge(ch, link.n)
                for j in range(HP):
                    step(v.max(sv[:, j // 2, j % 2, 8:K], rest[:, j, :]))
                dve.wait_ge(ch, link.n)
                for j in range(HP):
                    step(v.max_index(si[:, j // 2, j % 2, 8:K], sv[:, j // 2, j % 2, 8:K], rest[:, j, :]))
                dve.wait_ge(ch, link.n)
                v.tensor_copy(sif[:], si[:]).then_inc(scores_used, 1)
                for h in range(PH):
                    step(v.tensor_tensor(cand[:, h], sv[:, h, 0, :].unsqueeze(2).to_broadcast([P, K, K]),
                                         sv[:, h, 1, :].unsqueeze(1).to_broadcast([P, K, K]), ALU.add))
                dve.wait_ge(ch, link.n)
                c2 = lambda a, h: a[:, h].rearrange("p a b -> p (a b)")
                for h in range(PH):
                    step(v.max(cv[:, h, 0:8], c2(cand, h)))
                dve.wait_ge(ch, link.n)
                for h in range(PH):
                    step(v.max_index(ci[:, h, 0:8], cv[:, h, 0:8], c2(cand, h)))
                    step(v.match_replace(c2(crest, h), cv[:, h, 0:8], c2(cand, h), LOWEST))
                dve.wait_ge(ch, link.n)
                for h in range(PH):
                    step(v.max(cv[:, h, 8:K], c2(crest, h)))
                dve.wait_ge(ch, link.n)
                for h in range(PH):
                    step(v.max_index(ci[:, h, 8:K], cv[:, h, 8:K], c2(crest, h)))
                g = gate[t % 2]
                if t >= 2:
                    dve.wait_ge(turned, t - 1)
                v.tensor_tensor(g[:], cv[:], cv[:, :, 0:1].to_broadcast([P, PH, K]), ALU.subtract).then_inc(exp_in, 1)
                dve.wait_ge(ch, link.n)
                step(v.tensor_scalar(part[:, 0], ci[:], 4, None, ALU.logical_shift_right))
                link(v.tensor_scalar(part[:, 1], ci[:], K - 1, None, ALU.bitwise_and))
                link(v.tensor_copy(partf[:], part[:]))
                for half in range(2):
                    link(v.tensor_tensor(pick[:], partf[:, half].rearrange("p h k -> p (h k)").unsqueeze(2).to_broadcast([P, SLOTS, K]),
                                         iota[:].unsqueeze(1).to_broadcast([P, SLOTS, K]), ALU.is_equal))
                    p4 = pick[:].rearrange("p (h j) k -> p h j k", h=PH)
                    for h in range(PH):
                        step(v.tensor_tensor(p4[:, h], p4[:, h], sif[:, h, half, :].unsqueeze(1).to_broadcast([P, K, K]), ALU.mult))
                    dve.wait_ge(ch, link.n)
                    link(v.tensor_reduce(num[t % 2][:, half], pick[:], AX.X, ALU.add))
                dve.wait_ge(exp_done, t + 1)
                link(v.tensor_reduce(zsum[:], g[:], AX.X, ALU.add))
                link(v.reciprocal(zsum[:], zsum[:]))
                v.tensor_tensor(g[:], g[:], zsum[:].unsqueeze(2).to_broadcast([P, PH, K]), ALU.mult).then_inc(tile_done, 1)

        @block.scalar
        def _(act):
            for t in range(TILES):
                act.wait_ge(exp_in, t + 1)
                nc.scalar.activation(gate[t % 2][:], gate[t % 2][:], ACT.Exp).then_inc(exp_done, 1)
                act.wait_ge(turned, t + 1)
                nc.scalar.activation(core.slotT[:, :, t * P:(t + 1) * P], pt[t % 2][:], ACT.Copy).then_inc(turned_read, 1)

        @block.tensor
        def _(pe):
            for t in range(TILES):
                pe.wait_ge(tile_done, t + 1)
                if t >= 2:
                    pe.wait_ge(turned_read, t - 1)
                nc.tensor.transpose(pt[t % 2][:, 0, :], gate[t % 2][:].rearrange("p h k -> p (h k)"), core.ident[:])
                for half in range(2):
                    last = nc.tensor.transpose(pt[t % 2][:, 1 + half, :], num[t % 2][:, half], core.ident[:])
                last.then_inc(turned, 1)


def stage_gates(core):
    nc, dram = core.nc, core.dram
    TG = 4
    TURN = 2 * TG
    with Stage(core, "gates") as st:
        iota = st.sb("iota", [P, P])
        one = [st.sb(f"one{i}", [P, TG, P]) for i in range(2)]
        scaled = [st.sb(f"scaled{i}", [P, TG, P]) for i in range(2)]
        G = [st.sb(f"G{i}", [P, P, P]) for i in range(2)]
        pg = [st.psum(f"pg{i}", [P, TG, P]) for i in range(2)]
        iota_done = st.sem("iota_done")
        hot = st.sem("hot")
        used = st.sem("used")
        read = st.sem("read")
        g_out = [st.sem(f"g_out{i}") for i in range(2)]
        block = st.block()
        PER = P // TG

        @block.gpsimd
        def _(pool):
            nc.gpsimd.iota(iota[:], [[1, P]], base=0, channel_multiplier=0, allow_small_or_imprecise_dtypes=True)\
                .then_inc(iota_done, 1)

        @block.vector
        def _(dve):
            dve.wait_ge(iota_done, 1)
            with dve.Fori(0, T // TURN) as turn:
                for b in range(2):
                    dve.wait_ge(used, 2 * turn + (b + 1))
                    for j in range(TG):
                        slot = lambda which: core.slotT[:, which, bass.ds(turn * TURN + (b * TG + j), 1)]
                        nc.vector.tensor_scalar(one[b][:, j, :], iota[:], slot(2), None, ALU.is_equal)
                        last = nc.vector.tensor_scalar(scaled[b][:, j, :], iota[:], slot(1), slot(0), ALU.is_equal, ALU.mult)
                    last.then_inc(hot, 1)

        @block.tensor
        def _(pe):
            pe.sem_inc(used, 2)
            with pe.Fori(0, T // TURN) as turn:
                for b in range(2):
                    pe.wait_ge(hot, 2 * turn + (b + 1))
                    pe.wait_ge(read, 2 * turn + (b + 1))
                    for j in range(TG):
                        last = nc.tensor.matmul(pg[b][:, j, :], one[b][:, j, :], scaled[b][:, j, :], start=True, stop=True)
                    last.then_inc(used, 1)

        @block.scalar
        def _(act):
            act.sem_inc(read, 2)
            for t in range(TILES):
                if t >= 2:
                    act.wait_ge(g_out[t % 2], 16 * (t // 2))
                with act.Fori(0, P // TURN) as turn:
                    for b in range(2):
                        act.wait_ge(used, 2 * turn + (PER * t + b + 3))
                        nc.scalar.activation(G[t % 2][:, :, bass.ds(turn * TURN + b * TG, TG)],
                                             pg[b][:].rearrange("p t i -> p i t"), ACT.Copy).then_inc(read, 1)

        @block.sync
        def _(sp):
            for t in range(TILES):
                sp.wait_ge(read, PER * (t + 1) + 2)
                sp.dma_start(dram["gates"][:, :, t * P:(t + 1) * P].rearrange("a b t -> b a t"), G[t % 2][:])\
                    .then_inc(g_out[t % 2], 16)
            for i in range(2):
                sp.wait_ge(g_out[i], 16 * ((TILES + 1 - i) // 2))


def stage_split(core, xh, xl):
    nc, dram = core.nc, core.dram
    with Stage(core, "split") as st:
        h = [st.sb(f"h{i}", [P, T]) for i in range(4)]
        h_in = [st.sem(f"h_in{i}") for i in range(4)]
        high = st.sem("high")
        low = st.sem("low")
        block = st.block()

        @block.sync
        def _(sp):
            for k in range(KB):
                if k >= 4:
                    sp.wait_ge(low, k - 3)
                sp.dma_start(h[k % 4][:], dram["h2T"][:, k, :]).then_inc(h_in[k % 4], 16)

        @block.scalar
        def _(act):
            for k in range(KB):
                act.wait_ge(h_in[k % 4], 16 * (k // 4 + 1))
                nc.scalar.activation(xh[:, k, :], h[k % 4][:], ACT.Copy).then_inc(high, 1)

        @block.vector
        def _(dve):
            for k in range(KB):
                dve.wait_ge(high, k + 1)
                nc.vector.tensor_tensor(xl[:, k, :], h[k % 4][:], xh[:, k, :].bitcast(F32), ALU.subtract).then_inc(low, 1)


def stage_experts(core, xh, xl, y):
    nc, dram = core.nc, core.dram
    PAIRS = P // 2
    NY = TILES * 2
    YC = D // 2
    with Stage(core, "experts") as st:
        two = lambda name, shape, dt: [st.sb(f"{name}{i}", shape, dt) for i in range(2)]
        Ur, Uh, Ul = two("Ur", [P, KB, P], F32), two("Uh", [P, KB, P], F32R), two("Ul", [P, KB, P], F32R)
        Vr, Vh, Vl = two("Vr", [P, D], F32), two("Vh", [P, D], F32R), two("Vl", [P, D], F32R)
        G = two("G", [P, T], F32)
        tmp = [st.sb(f"tmp{c}", [P, TC], F32) for c in range(NTC)]
        Ch = [st.sb(f"Ch{i}", [P, T], F32R) for i in range(3)]
        Cl = [st.sb(f"Cl{i}", [P, T], F32R) for i in range(3)]
        pu = [st.psum(f"pu{c}", [P, 512]) for c in range(NTC)]
        pv = [st.psum(f"pv{i}", [P, YC]) for i in range(3)]
        u_in = [st.sem(f"u_in{j}") for j in range(2)]
        v_in = [st.sem(f"v_in{j}") for j in range(2)]
        g_in = [st.sem(f"g_in{j}") for j in range(2)]
        u_high, u_split, v_high, v_split = st.sem("u_high"), st.sem("u_split"), st.sem("v_high"), st.sem("v_split")
        u_made, gelu_done, gated, c_high, c_split = (st.sem(n) for n in ("u_made", "gelu_done", "gated", "c_high", "c_split"))
        v_made, y_added = st.sem("v_made"), st.sem("y_added")
        y_zero = st.sem("y_zero")
        block = st.block()

        def run(engine, step):
            step(-1, 1)
            step(0, 0)
            with engine.Fori(0, (PAIRS - 4) // 2) as i:
                step(2 * i + 1, 1)
                step(2 * i + 2, 0)
            step(PAIRS - 3, 1)
            step(PAIRS - 2, 0)
            step(PAIRS - 1, 1)

        def is_(s, *values):
            return isinstance(s, int) and s in values

        def slot(parity, j):
            return 2 if j == 1 else 1 - parity

        @block.sync
        def _(sp):
            def load(b, j, what, first=False):
                if what == "u":
                    if not first:
                        sp.wait_ge(u_split, b - 1)
                    sp.dma_start(Ur[j][:], dram["peer_u"][b]).then_inc(u_in[j], 16)
                elif what == "v":
                    if not first:
                        sp.wait_ge(v_split, b - 1)
                    sp.dma_start(Vr[j][:], dram["peer_v"][b]).then_inc(v_in[j], 16)
                else:
                    if not first:
                        sp.wait_ge(gated, 3 * (b - 1))
                    sp.dma_start(G[j][:], dram["gates"][b]).then_inc(g_in[j], 16)

            for j in range(2):
                load(j, j, "u", True)
                load(j, j, "g", True)

            def step(s, parity):
                if is_(s, PAIRS - 1):
                    return
                for j in range(2):
                    load(2 * s + 2 + j, j, "v", is_(s, -1))
                if is_(s, PAIRS - 2):
                    return
                for j in range(2):
                    load(2 * s + 4 + j, j, "u")
                    load(2 * s + 4 + j, j, "g")

            run(sp, step)

        @block.scalar
        def _(act):
            def high_u(b, j, s):
                act.wait_ge(u_in[j], 16 * (s + 1))
                if not is_(b, 0, 1):
                    act.wait_ge(u_made, 3 * (b - 1))
                nc.scalar.activation(Uh[j][:], Ur[j][:], ACT.Copy).then_inc(u_high, 1)

            def coefficients(b, j, s, parity):
                def high(c):
                    act.wait_ge(gated, 3 * b + (c + 1))
                    nc.scalar.activation(Ch[slot(parity, j)][:, c * TC:(c + 1) * TC], tmp[c][:], ACT.Copy).then_inc(c_high, 1)

                if j == 0 and not is_(s, -1, 0):
                    act.wait_ge(v_made, NY * s)
                if j == 1 and not is_(s, -1):
                    act.wait_ge(v_made, NY * (s + 1))
                for c in range(NTC):
                    act.wait_ge(u_made, 3 * b + (c + 1))
                    if not is_(b, 0):
                        act.wait_ge(c_split, 3 * (b - 1) + (c + 1))
                    nc.scalar.activation(tmp[c][:], pu[c][:, 0:TC], ACT.Gelu_apprx_tanh).then_inc(gelu_done, 1)
                    if c > 0:
                        high(c - 1)
                high(NTC - 1)

            high_u(0, 0, 0)
            high_u(1, 1, 0)

            def step(s, parity):
                if is_(s, PAIRS - 1):
                    return
                coefficients(2 * s + 2, 0, s, parity)
                if not is_(s, PAIRS - 2):
                    high_u(2 * s + 4, 0, s + 2)
                if not is_(s, -1):
                    act.wait_ge(v_made, NY * (s + 1))
                for j in range(2):
                    act.wait_ge(v_in[j], 16 * (s + 2))
                    nc.scalar.activation(Vh[j][:], Vr[j][:], ACT.Copy).then_inc(v_high, 1)
                coefficients(2 * s + 3, 1, s, parity)
                if not is_(s, PAIRS - 2):
                    high_u(2 * s + 5, 1, s + 2)

            run(act, step)

        @block.vector
        def _(dve):
            sub = lambda low, raw, high: nc.vector.tensor_tensor(low, raw, high.bitcast(F32), ALU.subtract)

            def low_u(b, j):
                dve.wait_ge(u_high, b + 1)
                sub(Ul[j][:], Ur[j][:], Uh[j][:]).then_inc(u_split, 1)

            def coefficients(b, j, s, parity):
                def low(c):
                    dve.wait_ge(c_high, 3 * b + (c + 1))
                    i, cols = slot(parity, j), slice(c * TC, (c + 1) * TC)
                    sub(Cl[i][:, cols], tmp[c][:], Ch[i][:, cols]).then_inc(c_split, 1)

                dve.wait_ge(g_in[j], 16 * (s + 2))
                for c in range(NTC):
                    dve.wait_ge(gelu_done, 3 * b + (c + 1))
                    nc.vector.tensor_tensor(tmp[c][:], tmp[c][:], G[j][:, c * TC:(c + 1) * TC], ALU.mult).then_inc(gated, 1)
                    if c > 0:
                        low(c - 1)
                low(NTC - 1)

            nc.vector.memset(y[:], 0.0).then_inc(y_zero, 1)
            dve.wait_ge(y_zero, 1)
            low_u(0, 0)
            low_u(1, 1)

            def step(s, parity):
                if not is_(s, PAIRS - 1):
                    coefficients(2 * s + 2, 0, s, parity)
                    if not is_(s, PAIRS - 2):
                        low_u(2 * s + 4, 0)
                if not is_(s, -1):
                    for r in range(NY):
                        dve.wait_ge(v_made, NY * s + (r + 1))
                        if not is_(s, 0):
                            dve.wait_ge(y_added, NY * (s - 1) + (r + 1))
                        dst = y[:, r // 2, (r % 2) * YC:(r % 2 + 1) * YC]
                        nc.vector.tensor_tensor(dst, dst, pv[r % 3][:], ALU.add).then_inc(y_added, 1)
                if is_(s, PAIRS - 1):
                    return
                for j in range(2):
                    dve.wait_ge(v_high, 2 * s + (3 + j))
                    sub(Vl[j][:], Vr[j][:], Vh[j][:]).then_inc(v_split, 1)
                coefficients(2 * s + 3, 1, s, parity)
                if not is_(s, PAIRS - 2):
                    low_u(2 * s + 5, 1)

            run(dve, step)

        @block.tensor
        def _(pe):
            mm = nc.tensor.matmul

            def products_u(b, j):
                pe.wait_ge(u_split, b + 1)
                for c in range(NTC):
                    if not is_(b, 0):
                        pe.wait_ge(gelu_done, 3 * (b - 1) + (c + 1))
                    cols = slice(c * TC, (c + 1) * TC)
                    for k in range(KB):
                        mm(pu[c][:, 0:TC], Uh[j][:, k, :], xh[:, k, cols], start=(k == 0), stop=False)
                        mm(pu[c][:, 0:TC], Uh[j][:, k, :], xl[:, k, cols], start=False, stop=False)
                        last = mm(pu[c][:, 0:TC], Ul[j][:, k, :], xh[:, k, cols], start=False, stop=(k == KB - 1))
                    last.then_inc(u_made, 1)

            def products_v(s, parity):
                pe.wait_ge(c_split, 6 * s + 6)
                pe.wait_ge(v_split, 2 * s + 2)
                for r in range(NY):
                    if not (is_(s, 0) and r < 3):
                        pe.wait_ge(y_added, NY * s + (r - 2))
                    t, cols = r // 2, slice((r % 2) * YC, (r % 2 + 1) * YC)
                    t = slice(t * P, (t + 1) * P)
                    for j in range(2):
                        i = 2 if j == 1 else parity
                        mm(pv[r % 3][:], Ch[i][:, t], Vh[j][:, cols], start=(j == 0), stop=False)
                        mm(pv[r % 3][:], Ch[i][:, t], Vl[j][:, cols], start=False, stop=False)
                        last = mm(pv[r % 3][:], Cl[i][:, t], Vh[j][:, cols], start=False, stop=(j == 1))
                    last.then_inc(v_made, 1)

            def step(s, parity):
                if not is_(s, PAIRS - 1):
                    products_u(2 * s + 2, 0)
                if not is_(s, -1):
                    products_v(s, parity)
                if not is_(s, PAIRS - 1):
                    products_u(2 * s + 3, 1)

            run(pe, step)


def stage_final(core, y):
    nc, dram = core.nc, core.dram
    with Stage(core, "final") as st:
        gate = st.sb("gate", [P, GROUPS, D])
        x = [st.sb(f"x{i}", [P, D]) for i in range(3)]
        sq = st.sb("sq", [P, D])
        ss = st.sb("ss", [P, TILES])
        rstd = st.sb("rstd", [P, TILES])
        gate_in = st.sem("gate_in")
        x_in = [st.sem(f"x_in{i}") for i in range(3)]
        squared = st.sem("squared")
        mean_done = st.sem("mean_done")
        root_done = st.sem("root_done")
        ch = st.sem("chain")
        y_done = st.sem("y_done")
        y_out = st.sem("y_out")
        block = st.block()

        @block.sync
        def _(sp):
            sp.dma_start(gate[:], dram["gate_rows"][1]).then_inc(gate_in, 16)
            for t in range(TILES):
                if t >= 3:
                    sp.wait_ge(y_done, t - 2)
                sp.dma_start(x[t % 3][:], dram["x1"][t * P:(t + 1) * P, :]).then_inc(x_in[t % 3], 16)

        @block.gpsimd
        def _(pool):
            for t in range(TILES):
                pool.wait_ge(y_done, t + 1)
                pool.dma_start(dram["y"][t * P:(t + 1) * P, :], y[:, t, :]).then_inc(y_out, 16)
            pool.wait_ge(y_out, 16 * TILES)

        @block.scalar
        def _(act):
            for t in range(TILES):
                if t > 0:
                    act.wait_ge(squared, t)
                nc.scalar.activation(sq[:], y[:, t, :], ACT.Square, accum_out=ss[:, t:t + 1]).then_inc(squared, 1)
            act.wait_ge(mean_done, 1)
            nc.scalar.activation(ss[:], rstd[:], ACT.Sqrt).then_inc(root_done, 1)

        @block.vector
        def _(dve):
            link = Chain(dve, ch)
            dve.wait_ge(squared, TILES)
            nc.vector.tensor_scalar(rstd[:], ss[:], 1.0 / D, EPS, ALU.mult, ALU.add).then_inc(mean_done, 1)
            dve.wait_ge(root_done, 1)
            link(nc.vector.reciprocal(rstd[:], ss[:]))
            dve.wait_ge(gate_in, 16)
            for t in range(TILES):
                link(nc.vector.scalar_tensor_tensor(out=y[:, t, :], in0=y[:, t, :], scalar=rstd[:, t:t + 1],
                                                    in1=gate[:, group_of(t), :], op0=ALU.mult, op1=ALU.mult))
                dve.wait_ge(x_in[t % 3], 16 * (t // 3 + 1))
                nc.vector.tensor_tensor(y[:, t, :], y[:, t, :], x[t % 3][:], ALU.add).then_inc(y_done, 1)


def build(nc, dram):
    dram["gate_rows"] = nc.dram_tensor("gate_rows", (2, P, GROUPS, D), F32).ap()
    dram["x1"] = nc.dram_tensor("x1", (T, D), F32).ap()
    dram["h2T"] = nc.dram_tensor("h2T", (P, KB, T), F32).ap()
    dram["scores"] = nc.dram_tensor("scores", (T, 2 * PH * P), F32).ap()
    dram["gates"] = nc.dram_tensor("gates", (P, P, T), F32).ap()
    with ExitStack() as stack:
        core = Core(nc, dram, stack)
        core.ident = core.keep("ident", [P, P])
        core.ones = core.keep("ones", [P, P])
        core.tri = core.keep("tri", [P, 2, P])
        core.shift_cols = core.keep("shift_cols", [P, 2, KB, GROUPS])
        core.scale_cols = core.keep("scale_cols", [P, 2, KB, GROUPS])
        stage_modulation(core)
        with Stage(core, "mixer") as mx:
            core.hT = mx.sb("hT", [P, KB, T])
            stage_norm(core, "norm1", dram["x"], 0)
            out = {n: mx.sb(n, [P, TILES, HW]) for n in ("q", "k", "v", "z")}
            out["guT"] = mx.sb("guT", [P, HEADS, T])
            for n in ("g", "beta", "neg_cum", "exp_cum", "exp_rest", "exp_tot"):
                out[n] = mx.sb(n, [P, TILES, UNITS])
            with Stage(core, "front") as fr:
                out["ab"] = fr.sb("ab", [P, TILES, 2 * UNITS])
                out["gv"] = fr.sb("gv", [P, TILES, HW])
                stage_project(core, out)
                stage_gmlp(core, out)
                stage_prepare(core, out)
            stage_scan(core, out)
            stage_out(core, out)
        with Stage(core, "retrieve") as rt:
            with Stage(core, "h2") as h2:
                core.hT = h2.sb("hT", [P, KB, T])
                stage_norm(core, "norm2", dram["x1"], 1)
                stage_queries(core, core.hT)
            core.slotT = rt.sb("slotT", [P, 3, T])
            stage_topk(core)
            stage_gates(core)
        with Stage(core, "peer") as pr:
            y = pr.sb("y", [P, TILES, D])
            xh = pr.sb("xh", [P, KB, T], F32R)
            xl = pr.sb("xl", [P, KB, T], F32R)
            stage_split(core, xh, xl)
            stage_experts(core, xh, xl, y)
            stage_final(core, y)


def constants():
    i = np.arange(P)
    tri = np.stack([i[:, None] <= i[None, :], i[:, None] >= i[None, :]], 1).astype(np.float32)
    far = np.stack([np.where(i[:, None] <= i[None, :], 0.0, FAR), np.where(i[:, None] >= i[None, :], 0.0, FAR)], 1)
    level = np.zeros((P, 2, LEVELS, P), np.float32)
    for l in range(LEVELS):
        b = 1 << l
        same = (i[:, None] // (2 * b)) == (i[None, :] // (2 * b))
        first = (i[:, None] // b) % 2 == 0
        level[:, 0, l] = same & first & ((i[None, :] // b) % 2 == 1)
        level[:, 1, l] = same & ~first & ((i[None, :] // b) % 2 == 0)
    n = np.arange((TILES - 1) * P)
    inv = (np.float32(10000.0) ** (-np.arange(32, dtype=np.float32) / np.float32(32))).astype(np.float32)
    row = (n // 64).astype(np.float32)[:, None] * inv
    col = (n % 64).astype(np.float32)[:, None] * inv
    cos = np.concatenate([np.cos(row), np.cos(row), np.cos(col), np.cos(col)], 1)
    sin = np.concatenate([-np.sin(row), np.sin(row), -np.sin(col), np.sin(col)], 1)
    tok = lambda a: np.ascontiguousarray(a.astype(np.float32).reshape(TILES - 1, P, P).transpose(1, 0, 2))
    return {"tri": tri, "far_masks": far.astype(np.float32), "level_masks": level, "rope_cos": tok(cos), "rope_sin": tok(sin)}


def lay_out(i):
    a = {k: np.asarray(v) for k, v in i.items()}
    blocks = lambda w: w.reshape(-1, P, w.shape[-1]).transpose(1, 0, 2)
    cols = lambda v: v.reshape(-1, P).T
    d = {}
    d["x"] = np.concatenate([a["x_prompt"].reshape(-1, D), a["x_sample"].reshape(-1, D)])
    d["c_cols"] = np.stack([cols(a["c_ctx"]), cols(a["c"][0])], 2)
    d["w_mod"] = blocks(a["w_mod"][0])
    b = a["b_mod"][0]
    d["b_mod_cols"] = cols(b)
    d["b_gate_rows"] = np.stack([b[2 * D:3 * D], b[5 * D:6 * D]])
    d["g_pre_cols"] = np.stack([cols(a["g_pre_mix"][0]), cols(a["g_pre_ffn"][0])], 1)
    d["g_post_rows"] = np.stack([a["g_post_mix"][0], a["g_post_ffn"][0]])
    d["w_in"] = blocks(a["w_in"][0])
    d["w_out"] = blocks(a["w_out"][0])
    d["gm_ws"] = a["gm_ws"][0].transpose(2, 0, 1)
    d["gm_bs"] = a["gm_bs"][0]
    d["conv_taps"] = a["dn_conv"][0].reshape(3, 12, P).transpose(2, 0, 1)
    d["decay_rows"] = np.stack([a["dn_a_log"][0].reshape(-1), a["dn_dt_bias"][0].reshape(-1)])
    d["norm_row"] = a["dn_norm"][0]
    d["state"] = a["state_delta"][0, 0].transpose(0, 2, 1, 3)
    d["peer_wq"] = blocks(a["peer_wq"][0])
    d["peer_keys"] = a["peer_keys"][0].reshape(2 * PH, P, P).transpose(2, 0, 1)
    d["peer_u"] = a["peer_u"][0].reshape(P, P, KB, P).transpose(0, 3, 2, 1)
    d["peer_v"] = a["peer_v"][0].reshape(P, P, D)
    d.update(constants())
    return {k: np.ascontiguousarray(v) for k, v in d.items()}


def kernel(**inputs):
    import concourse.bacc as bacc
    from concourse.bass_utils import run_bass_kernel_spmd

    nc = bacc.Bacc("TRN2", target_bir_lowering=False, num_devices=1)
    arrays = {f"in_{n}": a for n, a in lay_out(inputs).items()}
    dram = {n[3:]: nc.dram_tensor(n, a.shape, F32, kind="ExternalInput").ap() for n, a in arrays.items()}
    for n in ("b_gate_rows", "g_post_rows", "gm_bs", "decay_rows"):
        dram[n] = dram[n].unsqueeze(0)
    dram["norm_row"] = dram["norm_row"].unsqueeze(0)
    dram["y"] = nc.dram_tensor("out_y", (T, D), F32, kind="ExternalOutput").ap()
    dram["new_state"] = nc.dram_tensor("out_state", (2, P, HEADS, P), F32, kind="ExternalOutput").ap()
    build(nc, dram)
    r = run_bass_kernel_spmd(nc, [arrays], core_ids=[0]).results[0]
    y = r["out_y"]
    state = r["out_state"].transpose(0, 2, 1, 3)
    return (np.ascontiguousarray(y[:P].reshape(1, P, D)), np.ascontiguousarray(y[P:].reshape(1, T - P, D)),
            np.ascontiguousarray(state.reshape(1, 1, 2, HEADS, P, P)))
```

```python
from contextlib import ExitStack

import concourse.bass as bass
import numpy as np
from concourse import mybir

ALU = mybir.AluOpType
ACT = mybir.ActivationFunctionType
F32 = mybir.dt.float32
F32R = mybir.dt.float32r
U32 = mybir.dt.uint32
AX = mybir.AxisListType

P = 128
D = 1024
KB = D // P
TILES = 9
T = TILES * P
TC = 384
NTC = T // TC
HEADS = 4
HW = HEADS * P
UNITS = 8
GROUPS = 2
EPS = 1e-6
PH = 8
TOPK = 16
SLOTS = PH * TOPK
LEVELS = 7
FAR = -1e30
LOWEST = -3.0e38


def group_of(tile):
    return 0 if tile == 0 else 1


class Core:

    def __init__(self, nc, dram, stack):
        self.nc = nc
        self.dram = dram
        self.stack = stack
        self.sems = []

    def recycle_semaphores(self):
        self.nc.clear_and_free_semaphores(self.sems)
        self.nc.all_engine_barrier()
        self.sems = []

    def keep(self, name, shape, dt=F32):
        return self.stack.enter_context(self.nc.sbuf_tensor(name, shape, dt))


class Stage:

    def __init__(self, core, name):
        self.core = core
        self.nc, self.name, self.stack = core.nc, name, ExitStack()

    def sb(self, name, shape, dt=F32):
        return self.stack.enter_context(self.nc.sbuf_tensor(f"{self.name}_{name}", shape, dt))

    def psum(self, name, shape, dt=F32):
        return self.stack.enter_context(self.nc.psum_tensor(f"{self.name}_{name}", shape, dt))

    def sem(self, name):
        self.core.sems.append(self.nc.alloc_semaphore(f"{self.name}_{name}"))
        return self.core.sems[-1]

    def block(self):
        return self.stack.enter_context(self.nc.Block())

    def __enter__(self):
        return self

    def __exit__(self, *e):
        self.stack.close()


class Chain:

    def __init__(self, engine, sem):
        self.engine, self.sem, self.n = engine, sem, 0

    def __call__(self, ins):
        self.n += 1
        ins.then_inc(self.sem, 1)
        self.engine.wait_ge(self.sem, self.n)


SHIFT1, SCALE1, GATE1, SHIFT2, SCALE2, GATE2 = range(6)


class Modulation:

    def __init__(self, core, st, parts, width):
        self.core, self.parts, self.width = core, parts, width
        self.chunks = [(p, at) for p in parts for at in range(0, D, width)]
        self.ring = [st.sb(f"mod_w{i}", [P, KB, width]) for i in range(3)]
        self.bias = st.sb("mod_bias", [P, 6 * KB])
        self.gains = st.sb("mod_gains", [P, 2, 2, KB])
        self.sum = st.sb("mod_sum", [P, KB, GROUPS])
        self.cols = st.psum("mod_cols", [P, 512])
        self.small_in = st.sem("mod_small_in")
        self.w_in = [st.sem(f"mod_w_in{i}") for i in range(3)]
        self.used = st.sem("mod_used")
        self.chain = st.sem("mod_chain")

    def load(self, sp):
        sp.dma_start(self.bias[:], self.core.dram["b_mod_cols"]).then_inc(self.small_in, 16)
        sp.dma_start(self.gains[:], self.core.dram["gain_cols"]).then_inc(self.small_in, 16)
        for n, (part, at) in enumerate(self.chunks):
            if n >= 3:
                sp.wait_ge(self.used, n - 2)
            at += part * D
            sp.dma_start(self.ring[n % 3][:], self.core.dram["w_mod"][:, :, at:at + self.width]).then_inc(self.w_in[n % 3], 16)

    def products(self, pe, n):
        part, at = self.chunks[n]
        pe.wait_ge(self.w_in[n % 3], 16 * (n // 3 + 1))
        for b in range(self.width // P):
            j = part * KB + at // P + b
            for k in range(KB):
                last = self.core.nc.tensor.matmul(self.cols[:, j * GROUPS:(j + 1) * GROUPS],
                                                  self.ring[n % 3][:, k, b * P:(b + 1) * P], self.core.cact[:, k, :],
                                                  start=(k == 0), stop=(k == KB - 1))
        last.then_inc(self.used, 1)

    def finish(self, dve):
        v, core = self.core.nc.vector, self.core
        link = Chain(dve, self.chain)
        dve.wait_ge(self.small_in, 32)
        dve.wait_ge(self.used, len(self.chunks))
        for part in self.parts:
            which = part // 3
            src = self.cols[:, part * KB * GROUPS:(part + 1) * KB * GROUPS].rearrange("p (k g) -> p k g", g=GROUPS)
            bias = self.bias[:, part * KB:(part + 1) * KB].unsqueeze(2).to_broadcast([P, KB, GROUPS])
            gain = lambda post: self.gains[:, post, which, :].unsqueeze(2).to_broadcast([P, KB, GROUPS])
            if part in (SHIFT1, SHIFT2):
                link(v.tensor_tensor(core.shift_cols[:, which], src, bias, ALU.add))
                continue
            link(v.tensor_tensor(self.sum[:], src, bias, ALU.add))
            if part in (SCALE1, SCALE2):
                link(v.tensor_scalar(self.sum[:], self.sum[:], 1.0, None, ALU.add))
                link(v.tensor_tensor(core.scale_cols[:, which], self.sum[:], gain(0), ALU.mult))
            else:
                link(v.tensor_tensor(core.gate_cols[:, which], self.sum[:], gain(1), ALU.mult))


def spread_gates(core, which, bank, group):
    for k in range(KB):
        col = core.gate_cols[:, which, k, group:group + 1].to_broadcast([P, P])
        last = core.nc.tensor.matmul(bank[:, k * P:(k + 1) * P], col, core.ident[:], start=True, stop=True)
    return last


def stage_modulation(core):
    nc, dram = core.nc, core.dram
    with Stage(core, "mod") as st:
        mod = Modulation(core, st, (SHIFT1, SCALE1), 512)
        ccol = st.sb("ccol", [P, KB, GROUPS])
        c_in = st.sem("c_in")
        tri_in = st.sem("tri_in")
        act_done = st.sem("act_done")
        pool_chain = st.sem("pool_chain")
        block = st.block()

        @block.sync
        def _(sp):
            sp.dma_start(ccol[:], dram["c_cols"]).then_inc(c_in, 16)
            mod.load(sp)
            sp.dma_start(core.tri[:], dram["tri"]).then_inc(tri_in, 16)
            sp.wait_ge(tri_in, 16)

        @block.scalar
        def _(act):
            act.wait_ge(c_in, 16)
            nc.scalar.activation(core.cact[:], ccol[:], ACT.Silu).then_inc(act_done, 1)

        @block.gpsimd
        def _(pool):
            link = Chain(pool, pool_chain)
            link(nc.gpsimd.memset(core.ones[:], 1.0))
            link(nc.gpsimd.memset(core.ident[:], 0.0))
            link(nc.gpsimd.affine_select(out=core.ident[:], in_=core.ident[:], compare_op=ALU.not_equal, fill=1.0,
                                         base=0, pattern=[[-1, P]], channel_multiplier=1))

        @block.vector
        def _(dve):
            mod.finish(dve)

        @block.tensor
        def _(pe):
            pe.wait_ge(act_done, 1)
            for n in range(len(mod.chunks)):
                mod.products(pe, n)


def stage_norm(core, name, source, which):
    nc = core.nc
    BUFS = 3
    with Stage(core, name) as st:
        x = [st.sb(f"x{i}", [P, D]) for i in range(BUFS)]
        sq = st.sb("sq", [P, D])
        ss = st.sb("ss", [P, TILES])
        root = st.sb("root", [P, TILES])
        rstd = st.sb("rstd", [P, TILES])
        pt = [st.psum(f"pt{i}", [P, 4, P]) for i in range(4)]
        x_in = [st.sem(f"x_in{i}") for i in range(BUFS)]
        sq_done = st.sem("sq_done")
        mean_done = st.sem("mean_done")
        root_done = st.sem("root_done")
        recip_done = st.sem("recip_done")
        xn_done = st.sem("xn_done")
        turned = st.sem("turned")
        out_act = st.sem("out_act")
        out_dve = st.sem("out_dve")
        block = st.block()

        @block.sync
        def _(sp):
            for t in range(TILES):
                if t >= BUFS:
                    sp.wait_ge(turned, 2 * (t - BUFS + 1))
                sp.dma_start(x[t % BUFS][:], source[t * P:(t + 1) * P, :]).then_inc(x_in[t % BUFS], 16)

        @block.scalar
        def _(act):
            def evacuate(t):
                act.wait_ge(turned, 2 * t + 1)
                for j in range(4):
                    nc.scalar.activation(core.hT[:, j, t * P:(t + 1) * P], pt[(2 * t) % 4][:, j, :], ACT.Identity,
                                         bias=core.shift_cols[:, which, j, group_of(t):group_of(t) + 1],
                                         scale=core.scale_cols[:, which, j, group_of(t):group_of(t) + 1])\
                        .then_inc(out_act, 1)

            for t in range(TILES):
                act.wait_ge(x_in[t % BUFS], 16 * (t // BUFS + 1))
                if t > 0:
                    act.wait_ge(sq_done, t)
                nc.scalar.activation(sq[:], x[t % BUFS][:], ACT.Square, accum_out=ss[:, t:t + 1]).then_inc(sq_done, 1)
                act.wait_ge(mean_done, t + 1)
                nc.scalar.activation(root[:, t:t + 1], rstd[:, t:t + 1], ACT.Sqrt).then_inc(root_done, 1)
                if t > 0:
                    evacuate(t - 1)
            evacuate(TILES - 1)

        @block.vector
        def _(dve):
            def evacuate(t):
                dve.wait_ge(turned, 2 * t + 2)
                for j in range(4):
                    nc.vector.tensor_scalar(core.hT[:, 4 + j, t * P:(t + 1) * P], pt[(2 * t + 1) % 4][:, j, :],
                                            core.scale_cols[:, which, 4 + j, group_of(t):group_of(t) + 1],
                                            core.shift_cols[:, which, 4 + j, group_of(t):group_of(t) + 1],
                                            ALU.mult, ALU.add).then_inc(out_dve, 1)

            for t in range(TILES):
                r = rstd[:, t:t + 1]
                dve.wait_ge(sq_done, t + 1)
                nc.vector.tensor_scalar(r, ss[:, t:t + 1], 1.0 / D, EPS, ALU.mult, ALU.add).then_inc(mean_done, 1)
                dve.wait_ge(root_done, t + 1)
                nc.vector.reciprocal(r, root[:, t:t + 1]).then_inc(recip_done, 1)
                dve.wait_ge(recip_done, t + 1)
                nc.vector.tensor_scalar(x[t % BUFS][:], x[t % BUFS][:], r, None, ALU.mult).then_inc(xn_done, 1)
                if t > 0:
                    evacuate(t - 1)
            evacuate(TILES - 1)

        @block.tensor
        def _(pe):
            for t in range(TILES):
                pe.wait_ge(xn_done, t + 1)
                if t >= 2:
                    pe.wait_ge(out_act, 4 * (t - 1))
                    pe.wait_ge(out_dve, 4 * (t - 1))
                for half in range(2):
                    for j in range(4):
                        k = 4 * half + j
                        last = nc.tensor.transpose(pt[(2 * t + half) % 4][:, j, :], x[t % BUFS][:, k * P:(k + 1) * P],
                                                   core.ident[:])
                    last.then_inc(turned, 1)


def stage_project(core, out):
    nc, dram = core.nc, core.dram
    CW = 256
    GU, GV, QKV, Z = 0, 512, 1024, 2560
    cols = list(range(GU, 1024, CW)) + list(range(QKV, 3072, CW))
    AB = 2 * UNITS
    RAW = T + 4
    PAD = [0, P + 1, P + 2, T + 3]

    def spans(c):
        a, b = c * TC, (c + 1) * TC
        return [(0, P, 1), (P, b, P + 3)] if c == 0 else [(a, b, a + 3)]

    with Stage(core, "proj") as st:
        w = [st.sb(f"w{i}", [P, KB, CW]) for i in range(2)]
        wab = st.sb("wab", [P, KB, AB])
        raw = [st.sb(f"raw{i}", [P, RAW]) for i in range(2)]
        conv = [st.sb(f"conv{i}", [P, RAW]) for i in range(2)]
        taps = st.sb("taps", [P, 3, 12])
        pf = [st.psum(f"pf{i}", [P, 512]) for i in range(4)]
        pt = [st.psum(f"pt{i}", [P, 4, P]) for i in range(4)]
        small_in = st.sem("small_in")
        w_in = [st.sem(f"w_in{i}") for i in range(2)]
        pads = st.sem("pads")
        made = st.sem("made")
        read = st.sem("read")
        conv_done = st.sem("conv_done")
        silu_done = st.sem("silu_done")
        dve_chain = st.sem("dve_chain")
        turned = st.sem("turned")
        turned_read = st.sem("turned_read")
        block = st.block()

        jobs = []
        for n, at in enumerate(cols):
            if at < GV or QKV <= at < Z:
                for b in range(CW // P):
                    f = (at + b * P - (GU if at < GV else QKV)) // P
                    for c in range(NTC):
                        jobs.append(("gu" if at < GV else "qkv", f, c, n, b))
            else:
                for t in range(TILES):
                    jobs.append(("gv" if at < QKV else "z", t, (at - (GV if at < QKV else Z)) // CW, n, 0))
        for t in range(TILES):
            jobs.append(("ab", t, 0, len(cols), 0))
        qkv_read = {}
        for i, (kind, f, c, n, b) in enumerate(jobs):
            if kind == "qkv" and c == NTC - 1:
                qkv_read[f] = i + 1

        last_job = {n: i for i, (kind, f, c, n, b) in enumerate(jobs)}

        @block.sync
        def _(sp):
            sp.dma_start(taps[:], dram["conv_taps"]).then_inc(small_in, 16)
            sp.dma_start(wab[:], dram["w_in"][:, :, 3072:3072 + AB]).then_inc(small_in, 16)
            for n, at in enumerate(cols):
                if n >= 2:
                    sp.wait_ge(made, last_job[n - 2] + 1)
                sp.dma_start(w[n % 2][:], dram["w_in"][:, :, at:at + CW]).then_inc(w_in[n % 2], 16)

        @block.tensor
        def _(pe):
            def turn(f):
                pe.wait_ge(silu_done, f + 1)
                for q in range(3):
                    r = 3 * f + q
                    if r >= 4:
                        pe.wait_ge(turned_read, r - 3)
                    for t in range(4 * q, min(4 * q + 4, TILES)):
                        at = t * P + (1 if t == 0 else 3)
                        last = nc.tensor.transpose(pt[r % 4][:, t - 4 * q, :], conv[f % 2][:, at:at + P], core.ident[:])
                    last.then_inc(turned, 1)

            seen = -1
            for i, (kind, f, c, n, b) in enumerate(jobs):
                if n != seen:
                    if n < len(cols):
                        pe.wait_ge(w_in[n % 2], 16 * (n // 2 + 1))
                    else:
                        pe.wait_ge(small_in, 2 * 16)
                    seen = n
                if i >= 4:
                    pe.wait_ge(read, i - 3)
                for k in range(KB):
                    if kind in ("gu", "qkv"):
                        dst, lhsT, rhs = pf[i % 4][:, 0:TC], w[n % 2][:, k, b * P:(b + 1) * P], core.hT[:, k, c * TC:(c + 1) * TC]
                    elif kind == "ab":
                        dst, lhsT, rhs = pf[i % 4][:, 0:AB], core.hT[:, k, f * P:(f + 1) * P], wab[:, k, :]
                    else:
                        dst, lhsT, rhs = pf[i % 4][:, 0:CW], core.hT[:, k, f * P:(f + 1) * P], w[n % 2][:, k, :]
                    last = nc.tensor.matmul(dst, lhsT, rhs, start=(k == 0), stop=(k == KB - 1))
                last.then_inc(made, 1)
                if kind == "qkv" and c == NTC - 1 and f >= 1:
                    turn(f - 1)
                if kind == "z" and f == 0 and c == 0:
                    turn(11)

        @block.scalar
        def _(act):
            def silu(f):
                act.wait_ge(conv_done, f + 1)
                nc.scalar.activation(conv[f % 2][:, 1:RAW - 1], conv[f % 2][:, 1:RAW - 1], ACT.Silu).then_inc(silu_done, 1)

            for i, (kind, f, c, n, b) in enumerate(jobs):
                act.wait_ge(made, i + 1)
                src = pf[i % 4]
                if kind == "gu":
                    nc.scalar.activation(out["guT"][:, f, c * TC:(c + 1) * TC], src[:, 0:TC], ACT.Gelu_apprx_tanh).then_inc(read, 1)
                elif kind == "gv":
                    nc.scalar.activation(out["gv"][:, f, c * CW:(c + 1) * CW], src[:, 0:CW], ACT.Gelu_apprx_tanh).then_inc(read, 1)
                elif kind == "z":
                    nc.scalar.activation(out["z"][:, f, c * CW:(c + 1) * CW], src[:, 0:CW], ACT.Silu).then_inc(read, 1)
                elif kind == "ab":
                    nc.scalar.activation(out["ab"][:, f, :], src[:, 0:AB], ACT.Copy).then_inc(read, 1)
                else:
                    if c == 0 and f >= 2:
                        act.wait_ge(conv_done, f - 1)
                    for a, e, at in spans(c):
                        ins = nc.scalar.activation(raw[f % 2][:, at:at + e - a], src[:, a - c * TC:e - c * TC], ACT.Copy)
                    ins.then_inc(read, 1)
                    if c == NTC - 1 and f >= 1:
                        silu(f - 1)
                if kind == "z" and f == 0 and c == 0:
                    silu(11)

        @block.vector
        def _(dve):
            for i in range(2):
                for at in PAD:
                    nc.vector.memset(raw[i][:, at:at + 1], 0.0).then_inc(pads, 1)
            dve.wait_ge(small_in, 2 * 16)
            dve.wait_ge(pads, 2 * len(PAD))
            link = Chain(dve, dve_chain)
            dst = [out["q"], out["k"], out["v"]]

            def convolve(f):
                dve.wait_ge(read, qkv_read[f])
                r, o = raw[f % 2], conv[f % 2]
                if f >= 2:
                    dve.wait_ge(turned, 3 * (f - 1))
                o = o[:, 1:RAW - 1]
                link(nc.vector.tensor_scalar(o, r[:, 0:RAW - 2], taps[:, 0, f:f + 1], None, ALU.mult))
                link(nc.vector.scalar_tensor_tensor(out=o, in0=r[:, 1:RAW - 1], scalar=taps[:, 1, f:f + 1], in1=o,
                                                    op0=ALU.mult, op1=ALU.add))
                nc.vector.scalar_tensor_tensor(out=o, in0=r[:, 2:RAW], scalar=taps[:, 2, f:f + 1], in1=o,
                                               op0=ALU.mult, op1=ALU.add).then_inc(conv_done, 1)

            def place(f):
                for q in range(3):
                    dve.wait_ge(turned, 3 * f + q + 1)
                    n = min(4, TILES - 4 * q)
                    nc.vector.tensor_copy(dst[f // 4][:, 4 * q:4 * q + n, (f % 4) * P:(f % 4 + 1) * P],
                                          pt[(3 * f + q) % 4][:, 0:n, :]).then_inc(turned_read, 1)

            for f in range(12):
                convolve(f)
                if f >= 1:
                    place(f - 1)
            place(11)


def stage_gmlp(core, out):
    nc, dram = core.nc, core.dram
    with Stage(core, "gmlp") as st:
        ws = st.sb("ws", [P, HEADS, P])
        bs = st.sb("bs", [P, HEADS, P])
        sq = [st.sb(f"sq{i}", [P, HEADS, P]) for i in range(2)]
        ss = st.sb("ss", [P, TILES, HEADS])
        rstd = st.sb("rstd", [P, TILES, HEADS])
        tmp = [st.sb(f"tmp{i}", [P, HEADS, P]) for i in range(2)]
        ps = [st.psum(f"ps{i}", [P, HEADS, P]) for i in range(4)]
        small_in = st.sem("small_in")
        squared = st.sem("squared")
        summed = st.sem("summed")
        root_done = st.sem("root_done")
        normed = st.sem("normed")
        mixed = st.sem("mixed")
        mixed_read = st.sem("mixed_read")
        chain = st.sem("chain")
        block = st.block()
        gv, guT = out["gv"], out["guT"]

        @block.sync
        def _(sp):
            sp.dma_start(ws[:], dram["gm_ws"]).then_inc(small_in, 16)
            sp.dma_start(bs[:], dram["gm_bs"].to_broadcast([P, HEADS, P])).then_inc(small_in, 16)

        @block.scalar
        def _(act):
            for t in range(TILES):
                if t >= 2:
                    act.wait_ge(summed, t - 1)
                nc.scalar.activation(sq[t % 2][:], gv[:, t, :].rearrange("p (h d) -> p h d", h=HEADS), ACT.Square)\
                    .then_inc(squared, 1)
            act.wait_ge(summed, TILES + 1)
            nc.scalar.activation(ss[:], rstd[:], ACT.Sqrt).then_inc(root_done, 1)

        @block.vector
        def _(dve):
            link = Chain(dve, chain)
            for t in range(TILES):
                dve.wait_ge(squared, t + 1)
                nc.vector.tensor_reduce(ss[:, t, :], sq[t % 2][:], AX.X, ALU.add).then_inc(summed, 1)
            dve.wait_ge(summed, TILES)
            nc.vector.tensor_scalar(rstd[:], ss[:], 1.0 / P, EPS, ALU.mult, ALU.add).then_inc(summed, 1)
            dve.wait_ge(root_done, 1)
            link(nc.vector.reciprocal(rstd[:], ss[:]))
            for t in range(TILES):
                v = gv[:, t, :].rearrange("p (h d) -> p h d", h=HEADS)
                r = rstd[:, t, :].unsqueeze(2).to_broadcast([P, HEADS, P])
                nc.vector.tensor_tensor(v, v, r, ALU.mult).then_inc(normed, 1)
            dve.wait_ge(small_in, 32)
            for t in range(TILES):
                dve.wait_ge(mixed, t + 1)
                g = guT[:, :, t * P:(t + 1) * P]
                if t >= 2:
                    dve.wait_ge(mixed_read, 2 * (t - 1))
                nc.vector.tensor_tensor(tmp[t % 2][:], ps[t % 4][:], bs[:], ALU.add).then_inc(mixed_read, 1)
                dve.wait_ge(mixed_read, 2 * t + 1)
                nc.vector.tensor_tensor(g, g, tmp[t % 2][:], ALU.mult).then_inc(mixed_read, 1)

        @block.tensor
        def _(pe):
            pe.wait_ge(small_in, 32)
            for t in range(TILES):
                pe.wait_ge(normed, t + 1)
                if t >= 4:
                    pe.wait_ge(mixed_read, 2 * (t - 4) + 1)
                for h in range(HEADS):
                    last = nc.tensor.matmul(ps[t % 4][:, h, :], gv[:, t, h * P:(h + 1) * P], ws[:, h, :], start=True, stop=True)
                last.then_inc(mixed, 1)


def stage_prepare(core, out):
    nc, dram = core.nc, core.dram
    q, k, ab = out["q"], out["k"], out["ab"]
    with Stage(core, "prep") as st:
        rope_c = st.sb("rope_c", [P, TILES - 1, P])
        rope_s = st.sb("rope_s", [P, TILES - 1, P])
        par = st.sb("par", [P, 2, UNITS])
        work = st.sb("work", [P, HW])
        work2 = st.sb("work2", [P, HW])
        ss = st.sb("ss", [P, TILES, 2, HEADS])
        rt = st.sb("rt", [P, TILES, 2, HEADS])
        x = st.sb("x", [P, TILES, UNITS])
        neg = st.sb("neg", [P, TILES, UNITS])
        low = st.sb("low", [P, TILES, UNITS])
        g = out["g"]
        beta = out["beta"]
        pg = st.psum("pg", [P, 512])
        pt = [st.psum(f"pt{i}", [P, 4, P]) for i in range(4)]
        mod = Modulation(core, st, (GATE1, SHIFT2, SCALE2, GATE2), 256)
        small_in = st.sem("small_in")
        ch = st.sem("chain")
        to_act = st.sem("to_act")
        from_act = st.sem("from_act")
        qk_done = st.sem("qk_done")
        turned = st.sem("turned")
        turned_read = st.sem("turned_read")
        sums_done = st.sem("sums_done")
        rest_done = st.sem("rest_done")
        block = st.block()

        @block.sync
        def _(sp):
            sp.dma_start(rope_c[:], dram["rope_cos"]).then_inc(small_in, 16)
            sp.dma_start(rope_s[:], dram["rope_sin"]).then_inc(small_in, 16)
            sp.dma_start(par[:], dram["decay_rows"].to_broadcast([P, 2, UNITS])).then_inc(small_in, 16)
            mod.load(sp)

        @block.vector
        def _(dve):
            link = Chain(dve, ch)
            dve.wait_ge(small_in, 48)
            a = ab[:, :, 0:UNITS]
            b = ab[:, :, UNITS:2 * UNITS]
            dt = par[:, 1, :].unsqueeze(1).to_broadcast([P, TILES, UNITS])
            link(nc.vector.tensor_tensor(x[:], a, dt, ALU.add))
            link(nc.vector.tensor_scalar(neg[:], x[:], -1.0, None, ALU.mult))
            link(nc.vector.tensor_tensor(low[:], x[:], neg[:], ALU.min))
            nc.vector.tensor_scalar(x[:], x[:], 0.0, None, ALU.max).then_inc(to_act, 1)
            for t in range(TILES):
                for j, src in enumerate((q, k)):
                    link(nc.vector.tensor_tensor(work[:], src[:, t, :], src[:, t, :], ALU.mult))
                    link(nc.vector.tensor_reduce(ss[:, t, j, :], work[:].rearrange("p (h d) -> p h d", h=HEADS), AX.X, ALU.add))
            nc.vector.tensor_scalar(ss[:], ss[:], EPS, None, ALU.add).then_inc(to_act, 1)
            dve.wait_ge(from_act, 4)
            link(nc.vector.tensor_scalar(beta[:], beta[:], 1.0, None, ALU.add))
            link(nc.vector.reciprocal(beta[:], beta[:]))
            link(nc.vector.tensor_tensor(x[:], x[:], low[:], ALU.add))
            rate = par[:, 0, :].unsqueeze(1).to_broadcast([P, TILES, UNITS])
            link(nc.vector.tensor_tensor(x[:], x[:], rate, ALU.mult))
            nc.vector.tensor_scalar(g[:], x[:], -1.0, None, ALU.mult).then_inc(to_act, 1)
            dve.wait_ge(from_act, 5)
            link(nc.vector.reciprocal(ss[:], rt[:]))
            link(nc.vector.tensor_scalar(ss[:, :, 0, :], ss[:, :, 0, :], float(P) ** -0.5, None, ALU.mult))
            for t in range(TILES):
                for j, src in enumerate((q, k)):
                    heads = src[:, t, :].rearrange("p (h d) -> p h d", h=HEADS)
                    r = ss[:, t, j, :].unsqueeze(2).to_broadcast([P, HEADS, P])
                    if t == 0:
                        nc.vector.tensor_tensor(heads, heads, r, ALU.mult).then_inc(qk_done, 1)
                        continue
                    link(nc.vector.tensor_tensor(heads, heads, r, ALU.mult))
                    cos = rope_c[:, t - 1, :].unsqueeze(1).to_broadcast([P, HEADS, P])
                    w3 = work[:].rearrange("p (h d) -> p h d", h=HEADS)
                    nc.vector.tensor_tensor(w3, heads, cos, ALU.mult).then_inc(ch, 1)
                    link.n += 1
                    s4 = src[:, t, :].rearrange("p (h e d) -> p h e d", h=2 * HEADS, e=2)
                    w4 = work2[:].rearrange("p (h e d) -> p h e d", h=2 * HEADS, e=2)
                    for e in range(2):
                        for half in range(2):
                            sin = rope_s[:, t - 1, half * 64 + e * 32:half * 64 + e * 32 + 32]
                            ins = nc.vector.tensor_tensor(w4[:, half::2, e, :], s4[:, half::2, 1 - e, :],
                                                          sin.unsqueeze(1).to_broadcast([P, HEADS, 32]), ALU.mult)
                            ins.then_inc(ch, 1)
                            link.n += 1
                    dve.wait_ge(ch, link.n)
                    nc.vector.tensor_tensor(src[:, t, :], work[:], work2[:], ALU.add).then_inc(qk_done, 1)
                    dve.wait_ge(qk_done, 2 * t + j + 1)
            mod.finish(dve)

        @block.scalar
        def _(act):
            act.wait_ge(small_in, 48)
            act.wait_ge(to_act, 1)
            nc.scalar.activation(low[:], low[:], ACT.Exp).then_inc(from_act, 1)
            nc.scalar.activation(par[:, 0, :], par[:, 0, :], ACT.Exp).then_inc(from_act, 1)
            nc.scalar.activation(beta[:], ab[:, :, UNITS:2 * UNITS], ACT.Exp, scale=-1.0).then_inc(from_act, 1)
            act.wait_ge(from_act, 1)
            nc.scalar.activation(low[:], low[:], ACT.Ln, bias=1.0).then_inc(from_act, 1)
            act.wait_ge(to_act, 2)
            nc.scalar.activation(rt[:], ss[:], ACT.Sqrt).then_inc(from_act, 1)
            act.wait_ge(sums_done, 1)
            cum = pg[:, 0:TILES * UNITS].rearrange("p (t u) -> p t u", t=TILES)
            tot = pg[:, 128:128 + TILES * UNITS].rearrange("p (t u) -> p t u", t=TILES)
            nc.scalar.activation(out["neg_cum"][:], cum, ACT.Copy, scale=-1.0).then_inc(from_act, 1)
            nc.scalar.activation(out["exp_cum"][:], cum, ACT.Exp)
            nc.scalar.activation(out["exp_tot"][:], tot, ACT.Exp)
            act.wait_ge(from_act, 6)
            nc.scalar.activation(x[:], tot, ACT.Copy).then_inc(from_act, 1)
            act.wait_ge(rest_done, 1)
            nc.scalar.activation(out["exp_rest"][:], out["exp_rest"][:], ACT.Exp)
            for i in range(2 * TILES):
                act.wait_ge(turned, i + 1)
                nc.scalar.activation(core.hT[:, 4 * (i % 2):4 * (i % 2) + 4, (i // 2) * P:(i // 2 + 1) * P], pt[i % 4][:],
                                     ACT.Copy).then_inc(turned_read, 1)

        @block.gpsimd
        def _(pool):
            pool.wait_ge(from_act, 7)
            nc.gpsimd.tensor_tensor(out["exp_rest"][:], x[:], out["neg_cum"][:], ALU.add).then_inc(rest_done, 1)

        @block.tensor
        def _(pe):
            chunks = len(mod.chunks)
            for n in range(chunks - TILES):
                mod.products(pe, n)
            pe.wait_ge(to_act, 3)
            for d in range(2):
                for src_m, base in ((core.tri[:, d, :], 0), (core.ones[:], 128)):
                    dst = pg[:, base:base + TILES * UNITS].rearrange("p (t u) -> p t u", t=TILES)[:, :, 4 * d:4 * d + 4]
                    last = nc.tensor.matmul(dst, src_m, g[:, :, 4 * d:4 * d + 4], start=True, stop=True)
            last.then_inc(sums_done, 1)
            for i in range(2 * TILES):
                t, src = i // 2, (q, k)[i % 2]
                pe.wait_ge(qk_done, i + 1)
                if i >= 4:
                    pe.wait_ge(turned_read, i - 3)
                for h in range(HEADS):
                    last = nc.tensor.transpose(pt[i % 4][:, h, :], src[:, t, h * P:(h + 1) * P], core.ident[:])
                last.then_inc(turned, 1)
                if i % 2 == 1:
                    mod.products(pe, chunks - TILES + t)


def stage_scan(core, out):
    nc, dram = core.nc, core.dram
    qT, kT = core.hT[:, 0:4, :], core.hT[:, 4:8, :]
    k, v, g, beta, o = out["k"], out["v"], out["g"], out["beta"], out["q"]
    tiles = [list(range(TILES)), [0] + list(range(TILES - 1, 0, -1))]
    S4 = [P, HEADS, P]
    NPE, NDVE, NACT, NPOOL = 17, 20, 8, 10

    pe_products = lambda n: NPE * n + 1
    pe_join = lambda n, l: NPE * n + (2 if l == 0 else 1 + 2 * l)
    pe_double = lambda n, l: NPE * n + 2 + 2 * l
    pe_w = lambda n: NPE * n + 15
    pe_u = lambda n: NPE * n + 16
    pe_o = lambda n: NPE * n + 17
    act_decay = lambda n: NACT * n + 1
    act_join = lambda n, l: NACT * n + 1 + l
    act_w = lambda n: NACT * n + 8
    dve_attn = lambda n: NDVE * n + 1
    dve_b = lambda n: NDVE * n + 2
    dve_r = lambda n, l: NDVE * n + 3 + 2 * l
    dve_v = lambda n, l: NDVE * n + 4 + 2 * l
    dve_new = lambda n: NDVE * n + 16
    dve_o1 = lambda n: NDVE * n + 17
    dve_s1 = lambda n: NDVE * n + 18
    dve_s2 = lambda n: NDVE * n + 19
    dve_o2 = lambda n: NDVE * n + 20
    pool_mask = lambda n, l: NPOOL * n + (1, 2, 4, 6, 7, 8, 9)[l]
    pool_ek = lambda n: NPOOL * n + 3
    pool_kd = lambda n: NPOOL * n + 5
    pool_o = lambda n: NPOOL * n + 10

    with Stage(core, "scan") as st:
        both = lambda name: [st.sb(f"{name}{s}", S4) for s in range(2)]
        level = st.sb("level", [P, 2, LEVELS, P])
        far = st.sb("far", [P, 2, P])
        D, B, R, V = both("D"), both("B"), both("R"), both("V")
        Z = [[st.sb(f"Z{s}{l}", S4) for l in range(1, LEVELS)] for s in range(2)]
        M = [[st.sb(f"M{s}{i}", S4) for i in range(2)] for s in range(2)]
        attn, ek, kd = both("attn"), both("ek"), both("kd")
        nW, new = [M[s][1] for s in range(2)], [M[s][0] for s in range(2)]
        osum = D
        S = [[st.sb(f"S{s}{i}", S4) for i in range(2)] for s in range(2)]
        bank = [[st.psum(f"b{s}{i}", S4) for i in range(4)] for s in range(2)]
        small_in = st.sem("small_in")
        cleared = st.sem("cleared")
        z_cleared = st.sem("z_cleared")
        states_out = st.sem("states_out")
        pe_s = [st.sem(f"pe{s}") for s in range(2)]
        act_s = [st.sem(f"act{s}") for s in range(2)]
        dve_s = [st.sem(f"dve{s}") for s in range(2)]
        pool_s = [st.sem(f"pool{s}") for s in range(2)]
        block = st.block()

        def wide(col):
            return col.unsqueeze(2).to_broadcast(S4)

        def at(x, s, c):
            return x[:, c, 4 * s:4 * s + 4]

        def heads(x, c):
            return x[:, c, :].rearrange("p (h d) -> p h d", h=HEADS)

        def joined(x, l, which):
            if len(x.shape) == 3:
                return x.rearrange("p h (n two b) -> p (h n) two b", two=2, b=1 << l)[:, :, which, :]
            return x.rearrange("p (n two b) -> p n two b", two=2, b=1 << l)[:, :, which, :]

        half = lambda x, l, which: joined(x, l, which) if l >= 5 else x
        ident4 = core.ident[:].unsqueeze(1).to_broadcast(S4)

        @block.sync
        def _(sp):
            sp.dma_start(level[:], dram["level_masks"]).then_inc(small_in, 16)
            sp.dma_start(far[:], dram["far_masks"]).then_inc(small_in, 16)
            for s in range(2):
                sp.dma_start(S[s][1][:], dram["state"][s]).then_inc(small_in, 16)
            for s in range(2):
                sp.wait_ge(dve_s[s], dve_s2(0))
                sp.dma_start(dram["new_state"][s], S[s][0][:]).then_inc(states_out, 16)
            sp.wait_ge(states_out, 32)

        @block.gpsimd
        def _(pool):
            nc.gpsimd.memset(o[:], 0.0).then_inc(cleared, 1)
            for s in range(2):
                nc.gpsimd.memset(S[s][0][:], 0.0).then_inc(cleared, 1)
            pool.wait_ge(cleared, 3)
            pool.wait_ge(small_in, 64)
            for n in range(TILES):
                for l in range(LEVELS):
                    for s in range(2):
                        c = tiles[s][n]
                        if l == 0:
                            pool.wait_ge(dve_s[s], dve_b(n))
                            if n > 0:
                                pool.wait_ge(pe_s[s], pe_join(n - 1, LEVELS - 1))
                        elif l >= 2:
                            pool.wait_ge(pe_s[s], pe_join(n, l - 2))
                            if l == 2:
                                pool.wait_ge(dve_s[s], dve_r(n, 0))
                        elif n > 0:
                            pool.wait_ge(pe_s[s], pe_join(n - 1, LEVELS - 2))
                        m = level[:, s, l, :].unsqueeze(1).to_broadcast(S4)
                        nc.gpsimd.tensor_tensor(M[s][l % 2][:], B[s][:], m, ALU.mult).then_inc(pool_s[s], 1)
                        if l == 1:
                            if n > 0:
                                pool.wait_ge(pe_s[s], pe_w(n - 1))
                            nc.gpsimd.tensor_tensor(ek[s][:], heads(k, c), wide(at(out["exp_cum"], s, c)), ALU.mult)\
                                .then_inc(pool_s[s], 1)
                        if l == 2:
                            if n > 0:
                                pool.wait_ge(pe_s[s], pe_o(n - 1))
                            nc.gpsimd.tensor_tensor(kd[s][:], heads(k, c), wide(at(out["exp_rest"], s, c)), ALU.mult)\
                                .then_inc(pool_s[s], 1)
                for s in range(2):
                    c = tiles[s][n]
                    pool.wait_ge(dve_s[s], dve_o2(n))
                    if s == 1:
                        pool.wait_ge(pool_s[0], pool_o(n))
                    elif n > 0:
                        pool.wait_ge(pool_s[1], pool_o(n - 1))
                    nc.gpsimd.tensor_tensor(heads(o, c), heads(o, c), osum[s][:], ALU.add).then_inc(pool_s[s], 1)

        @block.scalar
        def _(act):
            act.wait_ge(z_cleared, 2 * (LEVELS - 1))
            for n in range(TILES):
                for s in range(2):
                    c = tiles[s][n]
                    act.wait_ge(pe_s[s], pe_products(n))
                    if n > 0:
                        act.wait_ge(pool_s[s], pool_o(n - 1))
                    for h in range(HEADS):
                        ins = nc.scalar.activation(D[s][:, h, :], bank[s][2][:, h, :], ACT.Exp,
                                                   bias=out["neg_cum"][:, c, 4 * s + h:4 * s + h + 1])
                    ins.then_inc(act_s[s], 1)
                for l in range(1, LEVELS):
                    for s in range(2):
                        act.wait_ge(pe_s[s], pe_join(n, l))
                        nc.scalar.activation(joined(Z[s][l - 1][:], l, s), joined(bank[s][0][:], l, s), ACT.Copy)\
                            .then_inc(act_s[s], 1)
                for s in range(2):
                    act.wait_ge(pe_s[s], pe_w(n))
                    nc.scalar.activation(nW[s][:], bank[s][0][:], ACT.Copy, scale=-1.0).then_inc(act_s[s], 1)

        @block.vector
        def _(dve):
            for s in range(2):
                for l in range(1, LEVELS):
                    nc.vector.memset(Z[s][l - 1][:], 0.0).then_inc(z_cleared, 1)
            for n in range(TILES):
                for s in range(2):
                    c = tiles[s][n]
                    dve.wait_ge(act_s[s], act_decay(n))
                    nc.vector.tensor_tensor(attn[s][:], bank[s][1][:], D[s][:], ALU.mult).then_inc(dve_s[s], 1)
                    for h in range(HEADS):
                        ins = nc.vector.scalar_tensor_tensor(out=B[s][:, h, :], in0=bank[s][0][:, h, :],
                                                             scalar=beta[:, c, 4 * s + h:4 * s + h + 1], in1=D[s][:, h, :],
                                                             op0=ALU.mult, op1=ALU.mult)
                    ins.then_inc(dve_s[s], 1)
                for s in range(2):
                    dve.wait_ge(pool_s[s], pool_mask(n, 0))
                    nc.vector.tensor_tensor(R[s][:], ident4, M[s][0][:], ALU.subtract).then_inc(dve_s[s], 1)
                    dve.wait_ge(pe_s[s], pe_join(n, 0))
                    nc.vector.tensor_tensor(V[s][:], ident4, bank[s][0][:], ALU.subtract).then_inc(dve_s[s], 1)
                for l in range(1, LEVELS):
                    for s in range(2):
                        dve.wait_ge(pe_s[s], pe_double(n, l))
                        dve.wait_ge(dve_s[s], dve_r(n, l - 1))
                        r = joined(R[s][:], l, 1 - s)
                        nc.vector.tensor_tensor(r, r, joined(bank[s][2][:], l, 1 - s), ALU.subtract).then_inc(dve_s[s], 1)
                        if l < LEVELS - 1:
                            dve.wait_ge(dve_s[s], dve_v(n, l - 1))
                            x = joined(V[s][:], l, s)
                            nc.vector.tensor_tensor(x, x, joined(bank[s][1][:], l, s), ALU.subtract).then_inc(dve_s[s], 1)
                for s in range(2):
                    c = tiles[s][n]
                    dve.wait_ge(pe_s[s], pe_u(n))
                    nc.vector.tensor_tensor(new[s][:], bank[s][1][:], wide(at(beta, s, c)), ALU.mult).then_inc(dve_s[s], 1)
                for s in range(2):
                    c = tiles[s][n]
                    state = S[s][0 if n == 0 else 1]
                    dve.wait_ge(pe_s[s], pe_o(n))
                    nc.vector.tensor_tensor(osum[s][:], bank[s][2][:], wide(at(out["exp_cum"], s, c)), ALU.mult)\
                        .then_inc(dve_s[s], 1)
                    nc.vector.tensor_tensor(state[:], state[:], wide(at(out["exp_tot"], s, c)), ALU.mult)\
                        .then_inc(dve_s[s], 1)
                    dve.wait_ge(dve_s[s], dve_s1(n))
                    nc.vector.tensor_tensor(state[:], state[:], bank[s][0][:], ALU.add).then_inc(dve_s[s], 1)
                    nc.vector.tensor_tensor(osum[s][:], osum[s][:], bank[s][3][:], ALU.add).then_inc(dve_s[s], 1)

        @block.tensor
        def _(pe):
            mm = nc.tensor.matmul
            pe.wait_ge(small_in, 64)
            pe.wait_ge(cleared, 3)
            pe.wait_ge(z_cleared, 2 * (LEVELS - 1))
            for n in range(TILES):
                for s in range(2):
                    c = tiles[s][n]
                    t = slice(c * P, (c + 1) * P)
                    b = bank[s]
                    if n > 0:
                        pe.wait_ge(dve_s[s], dve_o2(n - 1))
                    for h in range(HEADS):
                        mm(b[0][:, h, :], kT[:, h, t], kT[:, h, t], start=True, stop=True)
                    for h in range(HEADS):
                        mm(b[1][:, h, :], kT[:, h, t], qT[:, h, t], start=True, stop=True)
                    mm(b[2][:], core.ident[:], far[:, s, :].unsqueeze(1).to_broadcast(S4), start=True, stop=False)
                    for h in range(HEADS):
                        gcol = g[:, c, 4 * s + h:4 * s + h + 1].to_broadcast([P, P])
                        last = mm(b[2][:, h, :], gcol, core.tri[:, s, :], start=False, stop=(h == HEADS - 1))
                    last.then_inc(pe_s[s], 1)
                for s in range(2):
                    pe.wait_ge(pool_s[s], pool_mask(n, 0))
                    for h in range(HEADS):
                        last = mm(bank[s][0][:, h, :], M[s][0][:, h, :], core.ident[:], start=True, stop=True)
                    last.then_inc(pe_s[s], 1)
                for l in range(1, LEVELS):
                    for s in range(2):
                        pe.wait_ge(pool_s[s], pool_mask(n, l))
                        pe.wait_ge(dve_s[s], dve_v(n, l - 1))
                        for h in range(HEADS):
                            last = mm(half(bank[s][0][:, h, :], l, s), M[s][l % 2][:, h, :], half(V[s][:, h, :], l, s),
                                      start=True, stop=True)
                        last.then_inc(pe_s[s], 1)
                    for s in range(2):
                        pe.wait_ge(act_s[s], act_join(n, l))
                        for h in range(HEADS):
                            last = mm(half(bank[s][2][:, h, :], l, 1 - s), Z[s][l - 1][:, h, :], half(R[s][:, h, :], l, 1 - s),
                                      start=True, stop=True)
                        if l < LEVELS - 1:
                            for h in range(HEADS):
                                last = mm(half(bank[s][1][:, h, :], l, s), R[s][:, h, :], half(Z[s][l - 1][:, h, :], l, s),
                                          start=True, stop=True)
                        last.then_inc(pe_s[s], 1)
                for s in range(2):
                    pe.wait_ge(dve_s[s], dve_r(n, LEVELS - 1))
                    pe.wait_ge(pool_s[s], pool_ek(n))
                    for h in range(HEADS):
                        last = mm(bank[s][0][:, h, :], ek[s][:, h, :], R[s][:, h, :], start=True, stop=True)
                    last.then_inc(pe_s[s], 1)
                for s in range(2):
                    state = S[s][0 if n == 0 else 1]
                    pe.wait_ge(act_s[s], act_w(n))
                    for h in range(HEADS):
                        mm(bank[s][1][:, h, :], R[s][:, h, :], v[:, tiles[s][n], h * P:(h + 1) * P], start=True, stop=False)
                        last = mm(bank[s][1][:, h, :], nW[s][:, h, :], state[:, h, :], start=False, stop=True)
                    last.then_inc(pe_s[s], 1)
                for s in range(2):
                    c = tiles[s][n]
                    t = slice(c * P, (c + 1) * P)
                    state = S[s][0 if n == 0 else 1]
                    for h in range(HEADS):
                        mm(bank[s][2][:, h, :], qT[:, h, t], state[:, h, :], start=True, stop=True)
                    pe.wait_ge(dve_s[s], dve_new(n))
                    pe.wait_ge(pool_s[s], pool_kd(n))
                    for h in range(HEADS):
                        mm(bank[s][3][:, h, :], attn[s][:, h, :], new[s][:, h, :], start=True, stop=True)
                    for h in range(HEADS):
                        last = mm(bank[s][0][:, h, :], kd[s][:, h, :], new[s][:, h, :], start=True, stop=True)
                    last.then_inc(pe_s[s], 1)


def stage_out(core, out):
    nc, dram = core.nc, core.dram
    o, z, oaT, obT = out["q"], out["z"], out["guT"], core.hT[:, 0:HEADS, :]
    with Stage(core, "out") as st:
        wo = st.sb("wo", [P, KB, D])
        nrow = st.sb("nrow", [P, P])
        gate = st.sb("gate", [P, GROUPS, D])
        sq = [st.sb(f"sq{i}", [P, HW]) for i in range(2)]
        ss = st.sb("ss", [P, TILES, HEADS])
        rstd = st.sb("rstd", [P, TILES, HEADS])
        x = [st.sb(f"x{i}", [P, D]) for i in range(2)]
        y = [st.sb(f"y{i}", [P, D]) for i in range(2)]
        ysq = st.sb("ysq", [P, D])
        ys = st.sb("ys", [P, TILES])
        yr = st.sb("yr", [P, TILES])
        pt = [st.psum(f"pt{i}", [P, HEADS, P]) for i in range(2)]
        py = [st.psum(f"py{i}", [P, 2, HW]) for i in range(2)]
        small_in = st.sem("small_in")
        x_in = [st.sem(f"x_in{i}") for i in range(2)]
        x_out = [st.sem(f"x_out{i}") for i in range(2)]
        squared = st.sem("squared")
        summed = st.sem("summed")
        root_done = st.sem("root_done")
        o_chain = st.sem("o_chain")
        gated = st.sem("gated")
        turned = st.sem("turned")
        turned_read = st.sem("turned_read")
        gate_spread = st.sem("gate_spread")
        gate_read = st.sem("gate_read")
        y_done = st.sem("y_done")
        y_sq = st.sem("y_sq")
        y_root = st.sem("y_root")
        y_mean = st.sem("y_mean")
        y_chain = st.sem("y_chain")
        x1_done = st.sem("x1_done")
        block = st.block()

        @block.sync
        def _(sp):
            sp.dma_start(nrow[:], dram["norm_row"].to_broadcast([P, P])).then_inc(small_in, 16)
            sp.dma_start(wo[:], dram["w_out"]).then_inc(small_in, 16)
            for t in range(TILES):
                if t >= 2:
                    sp.wait_ge(x1_done, t - 1)
                sp.dma_start(x[t % 2][:], dram["x"][t * P:(t + 1) * P, :]).then_inc(x_in[t % 2], 16)

        @block.gpsimd
        def _(pool):
            for t in range(TILES):
                pool.wait_ge(x1_done, t + 1)
                pool.dma_start(dram["x1"][t * P:(t + 1) * P, :], y[t % 2][:]).then_inc(x_out[t % 2], 16)
            for i in range(2):
                pool.wait_ge(x_out[i], 16 * ((TILES + 1 - i) // 2))

        @block.scalar
        def _(act):
            def rms(t):
                act.wait_ge(y_done, t + 1)
                if t > 0:
                    act.wait_ge(y_sq, t)
                nc.scalar.activation(ysq[:], py[t % 2][:].rearrange("p a b -> p (a b)"), ACT.Square,
                                     accum_out=ys[:, t:t + 1]).then_inc(y_sq, 1)
                act.wait_ge(y_mean, t + 1)
                nc.scalar.activation(ys[:, t:t + 1], yr[:, t:t + 1], ACT.Sqrt).then_inc(y_root, 1)

            for g in range(GROUPS):
                act.wait_ge(gate_spread, g + 1)
                nc.scalar.activation(gate[:, g, :], py[g][:].rearrange("p a b -> p (a b)"), ACT.Copy).then_inc(gate_read, 1)
            for t in range(TILES):
                if t >= 2:
                    act.wait_ge(summed, t - 1)
                nc.scalar.activation(sq[t % 2][:], o[:, t, :], ACT.Square).then_inc(squared, 1)
            act.wait_ge(summed, TILES + 1)
            nc.scalar.activation(ss[:], rstd[:], ACT.Sqrt).then_inc(root_done, 1)
            for t in range(TILES):
                act.wait_ge(turned, t + 1)
                nc.scalar.activation(obT[:, :, t * P:(t + 1) * P], pt[t % 2][:], ACT.Copy).then_inc(turned_read, 1)
                if t > 0:
                    rms(t - 1)
            rms(TILES - 1)

        @block.vector
        def _(dve):
            for t in range(TILES):
                dve.wait_ge(squared, t + 1)
                nc.vector.tensor_reduce(ss[:, t, :], sq[t % 2][:].rearrange("p (h d) -> p h d", h=HEADS), AX.X,
                                        ALU.add).then_inc(summed, 1)
            dve.wait_ge(summed, TILES)
            nc.vector.tensor_scalar(rstd[:], ss[:], 1.0 / P, EPS, ALU.mult, ALU.add).then_inc(summed, 1)
            dve.wait_ge(root_done, 1)
            link = Chain(dve, o_chain)
            link(nc.vector.reciprocal(rstd[:], ss[:]))
            dve.wait_ge(small_in, 32)
            for t in range(TILES):
                zt = z[:, t, :].rearrange("p (h d) -> p h d", h=HEADS)
                ot = o[:, t, :].rearrange("p (h d) -> p h d", h=HEADS)
                link(nc.vector.tensor_tensor(zt, zt, nrow[:].unsqueeze(1).to_broadcast([P, HEADS, P]), ALU.mult))
                link(nc.vector.tensor_tensor(ot, ot, rstd[:, t, :].unsqueeze(2).to_broadcast([P, HEADS, P]), ALU.mult))
                nc.vector.tensor_tensor(ot, ot, zt, ALU.mult).then_inc(gated, 1)
            link = Chain(dve, y_chain)
            dve.wait_ge(gate_read, GROUPS)
            for t in range(TILES):
                r = yr[:, t:t + 1]
                dve.wait_ge(y_sq, t + 1)
                nc.vector.tensor_scalar(r, ys[:, t:t + 1], 1.0 / D, EPS, ALU.mult, ALU.add).then_inc(y_mean, 1)
                dve.wait_ge(y_root, t + 1)
                link(nc.vector.reciprocal(r, ys[:, t:t + 1]))
                if t >= 2:
                    dve.wait_ge(x_out[t % 2], 16 * (t // 2))
                link(nc.vector.scalar_tensor_tensor(out=y[t % 2][:], in0=py[t % 2][:].rearrange("p a b -> p (a b)"), scalar=r,
                                                    in1=gate[:, group_of(t), :], op0=ALU.mult, op1=ALU.mult))
                dve.wait_ge(x_in[t % 2], 16 * (t // 2 + 1))
                nc.vector.tensor_tensor(y[t % 2][:], y[t % 2][:], x[t % 2][:], ALU.add).then_inc(x1_done, 1)

        @block.tensor
        def _(pe):
            def project(t):
                pe.wait_ge(turned_read, t + 1)
                if t == 0:
                    pe.wait_ge(small_in, 32)
                if t < GROUPS:
                    pe.wait_ge(gate_read, t + 1)
                if t >= 2:
                    pe.wait_ge(x1_done, t - 1)
                for half in range(2):
                    for k in range(KB):
                        src = oaT[:, k, t * P:(t + 1) * P] if k < HEADS else obT[:, k - HEADS, t * P:(t + 1) * P]
                        last = nc.tensor.matmul(py[t % 2][:, half, :], src, wo[:, k, half * HW:(half + 1) * HW],
                                                start=(k == 0), stop=(k == KB - 1))
                last.then_inc(y_done, 1)

            for g in range(GROUPS):
                spread_gates(core, 0, py[g][:].rearrange("p a b -> p (a b)"), g).then_inc(gate_spread, 1)
            for t in range(TILES):
                pe.wait_ge(gated, t + 1)
                if t >= 2:
                    pe.wait_ge(turned_read, t - 1)
                for h in range(HEADS):
                    last = nc.tensor.transpose(pt[t % 2][:, h, :], o[:, t, h * P:(h + 1) * P], core.ident[:])
                last.then_inc(turned, 1)
                if t > 0:
                    project(t - 1)
            project(TILES - 1)


def stage_queries(core, hT, xh, xl):
    nc, dram = core.nc, core.dram
    HP = 2 * PH
    GH = 4
    CW = GH * P
    WC = CW // 2
    with Stage(core, "query") as st:
        w = [st.sb(f"w{i}", [P, KB, WC]) for i in range(2)]
        wh = [st.sb(f"wh{i}", [P, KB, WC], F32R) for i in range(2)]
        wl = [st.sb(f"wl{i}", [P, KB, WC], F32R) for i in range(2)]
        keys = st.sb("keys", [P, HP, P])
        q = st.sb("q", [P, GH, T])
        s = [st.sb(f"s{i}", [P, CW]) for i in range(2)]
        pq = [st.psum(f"pq{i}", [P, 512]) for i in range(4)]
        ps = [st.psum(f"ps{i}", [P, CW]) for i in range(4)]
        keys_in = st.sem("keys_in")
        w_in = [st.sem(f"w_in{i}") for i in range(2)]
        x_high, x_low, w_high, w_low = (st.sem(n) for n in ("x_high", "x_low", "w_high", "w_low"))
        q_made = st.sem("q_made")
        q_read = st.sem("q_read")
        s_made = st.sem("s_made")
        s_read = st.sem("s_read")
        s_out = [st.sem(f"s_out{i}") for i in range(2)]
        block = st.block()
        GR = HP // GH
        PERW = GH * NTC // 2
        WN = 2 * GR

        @block.sync
        def _(sp):
            for n in range(WN):
                if n >= 2:
                    sp.wait_ge(w_low, n - 1)
                sp.dma_start(w[n % 2][:], dram["peer_wq"][:, :, n * WC:(n + 1) * WC]).then_inc(w_in[n % 2], 16)
                if n == 1:
                    sp.dma_start(keys[:], dram["peer_keys"]).then_inc(keys_in, 16)

        @block.gpsimd
        def _(pool):
            i = 0
            for g in range(GR):
                for t in range(TILES):
                    pool.wait_ge(s_read, i + 1)
                    pool.dma_start(dram["scores"][t * P:(t + 1) * P, g * CW:(g + 1) * CW], s[i % 2][:]).then_inc(s_out[i % 2], 16)
                    i += 1
            for j in range(2):
                pool.wait_ge(s_out[j], 16 * (GR * TILES // 2))

        @block.scalar
        def _(act):
            def high(n):
                act.wait_ge(w_in[n % 2], 16 * (n // 2 + 1))
                if n >= 2:
                    act.wait_ge(q_made, PERW * (n - 1))
                nc.scalar.activation(wh[n % 2][:], w[n % 2][:], ACT.Copy).then_inc(w_high, 1)

            high(0)
            for c in range(NTC):
                cols = slice(c * TC, (c + 1) * TC)
                nc.scalar.activation(xh[:, :, cols], hT[:, :, cols], ACT.Copy).then_inc(x_high, 1)
            high(1)
            i = 0
            for g in range(GR):
                if g > 0:
                    act.wait_ge(s_made, TILES * g)
                for b in range(GH):
                    for c in range(NTC):
                        act.wait_ge(q_made, i + 1)
                        nc.scalar.activation(q[:, b, c * TC:(c + 1) * TC], pq[i % 4][:, 0:TC], ACT.Copy).then_inc(q_read, 1)
                        i += 1
                        if i % PERW == 0 and i // PERW + 1 < WN:
                            high(i // PERW + 1)

        @block.vector
        def _(dve):
            def low(n):
                dve.wait_ge(w_high, n + 1)
                nc.vector.tensor_tensor(wl[n % 2][:], w[n % 2][:], wh[n % 2][:].bitcast(F32), ALU.subtract).then_inc(w_low, 1)

            low(0)
            for c in range(NTC):
                cols = slice(c * TC, (c + 1) * TC)
                dve.wait_ge(x_high, c + 1)
                nc.vector.tensor_tensor(xl[:, :, cols], hT[:, :, cols], xh[:, :, cols].bitcast(F32), ALU.subtract).then_inc(x_low, 1)
            low(1)
            for g in range(GR):
                for t in range(TILES):
                    i = g * TILES + t
                    if t == 0 and g < GR - 1:
                        low(2 * g + 2)
                    if t == TILES - 1 and g < GR - 1:
                        low(2 * g + 3)
                    dve.wait_ge(s_made, i + 1)
                    if i >= 2:
                        dve.wait_ge(s_out[i % 2], 16 * (i // 2))
                    nc.vector.tensor_copy(s[i % 2][:], ps[i % 4][:]).then_inc(s_read, 1)

        @block.tensor
        def _(pe):
            mm = nc.tensor.matmul
            i = 0
            for g in range(GR):
                for b in range(GH):
                    n = 2 * g + b // 2
                    f = slice((b % 2) * P, (b % 2 + 1) * P)
                    pe.wait_ge(w_low, n + 1)
                    for c in range(NTC):
                        if g == 0 and b == 0:
                            pe.wait_ge(x_low, c + 1)
                        if i >= 4:
                            pe.wait_ge(q_read, i - 3)
                        cols = slice(c * TC, (c + 1) * TC)
                        dst = pq[i % 4][:, 0:TC]
                        for k in range(KB):
                            mm(dst, wl[n % 2][:, k, f], xh[:, k, cols], start=(k == 0), stop=False)
                            mm(dst, wh[n % 2][:, k, f], xl[:, k, cols], start=False, stop=False)
                            last = mm(dst, wh[n % 2][:, k, f], xh[:, k, cols], start=False, stop=(k == KB - 1))
                        last.then_inc(q_made, 1)
                        i += 1
                pe.wait_ge(q_read, i)
                if g == 0:
                    pe.wait_ge(keys_in, 16)
                for t in range(TILES):
                    j = g * TILES + t
                    if j >= 4:
                        pe.wait_ge(s_read, j - 3)
                    for b in range(GH):
                        last = mm(ps[j % 4][:, b * P:(b + 1) * P], q[:, b, t * P:(t + 1) * P], keys[:, g * GH + b, :],
                                  start=True, stop=True)
                    last.then_inc(s_made, 1)


class Ahead:

    def __init__(self, core, st, ring, first, xh, xl):
        self.nc, self.dram, self.ring, self.first, self.xh, self.xl = core.nc, core.dram, ring, first, xh, xl
        self.Ur = st.sb("Ur", [P, KB, P])
        self.Uh = [st.sb(f"Uh{i}", [P, KB, P], F32R) for i in range(ring)]
        self.Ul = [st.sb(f"Ul{i}", [P, KB, P], F32R) for i in range(ring)]
        self.act = [st.sb(f"act{c}", [P, TC]) for c in range(NTC)]
        self.pu = [st.psum(f"pu{c}", [P, 512]) for c in range(NTC)]
        self.u_in, self.u_high, self.u_split = st.sem("u_in"), st.sem("u_high"), st.sem("u_split")
        self.u_made, self.gelu_done = st.sem("u_made"), st.sem("gelu_done")
        self.act_out = [st.sem(f"act_out{c}") for c in range(NTC)]

    def load(self, sp, n):
        sp.wait_ge(self.u_split, n + 1)
        sp.dma_start(self.Ur[:], self.dram["peer_u"][n + self.first]).then_inc(self.u_in, 16)

    def store(self, sp, n):
        for c in range(NTC):
            sp.wait_ge(self.gelu_done, 3 * n + (c + 4))
            sp.dma_start(self.dram["acts"][n + self.first][:, c * TC:(c + 1) * TC], self.act[c][:]).then_inc(self.act_out[c], 16)

    def high(self, act, n, slot):
        act.wait_ge(self.u_in, 16 * (n + 1))
        act.wait_ge(self.u_made, 3 * (n + 1))
        self.nc.scalar.activation(self.Uh[slot][:], self.Ur[:], ACT.Copy).then_inc(self.u_high, 1)

    def gelu(self, act, n):
        for c in range(NTC):
            act.wait_ge(self.u_made, 3 * n + (c + 1 + 3 * self.ring))
            act.wait_ge(self.act_out[c], 16 * (n + 1))
            self.nc.scalar.activation(self.act[c][:], self.pu[c][:, 0:TC], ACT.Gelu_apprx_tanh).then_inc(self.gelu_done, 1)

    def low(self, dve, n, slot):
        dve.wait_ge(self.u_high, n + 1)
        self.nc.vector.tensor_tensor(self.Ul[slot][:], self.Ur[:], self.Uh[slot][:].bitcast(F32), ALU.subtract)\
            .then_inc(self.u_split, 1)

    def products(self, pe, n, slot, c, half=None):
        mm = self.nc.tensor.matmul
        if half in (None, 0):
            pe.wait_ge(self.u_split, n + 2)
            pe.wait_ge(self.gelu_done, 3 * n + (c + 1))
        cols = slice(c * TC, (c + 1) * TC)
        dst = self.pu[c][:, 0:TC]
        for k in {None: range(KB), 0: range(KB // 2), 1: range(KB // 2, KB)}[half]:
            mm(dst, self.Uh[slot][:, k, :], self.xh[:, k, cols], start=(k == 0), stop=False)
            mm(dst, self.Uh[slot][:, k, :], self.xl[:, k, cols], start=False, stop=False)
            last = mm(dst, self.Ul[slot][:, k, :], self.xh[:, k, cols], start=False, stop=(k == KB - 1))
        if half in (None, 1):
            last.then_inc(self.u_made, 1)

    def begin(self, pe=None, act=None, dve=None):
        if pe is not None:
            pe.sem_inc(self.u_made, 3 * self.ring)
        if act is not None:
            act.sem_inc(self.gelu_done, 3)
            for c in range(NTC):
                act.sem_inc(self.act_out[c], 16)
        if dve is not None:
            dve.sem_inc(self.u_split, 1)

    def stored(self, sp, blocks):
        for c in range(NTC):
            sp.wait_ge(self.act_out[c], 16 * (blocks + 1))


TOPK_AHEAD = 5
GATE_AHEAD = 3


def stage_topk(core, xh, xl):
    nc, dram = core.nc, core.dram
    K = TOPK
    HP = 2 * PH
    A = TOPK_AHEAD
    with Stage(core, "topk") as st:
        s = st.sb("s", [P, HP, P])
        rest = st.sb("rest", [P, HP, P])
        sv = st.sb("sv", [P, PH, 2, K])
        si = st.sb("si", [P, PH, 2, K], U32)
        sif = st.sb("sif", [P, PH, 2, K])
        cand = st.sb("cand", [P, PH, K, K])
        crest = st.sb("crest", [P, PH, K, K])
        cv = st.sb("cv", [P, PH, K])
        ci = st.sb("ci", [P, PH, K], U32)
        part = st.sb("part", [P, 2, PH, K], U32)
        partf = st.sb("partf", [P, 2, PH, K])
        pick = st.sb("pick", [P, SLOTS, K])
        gate = st.sb("gate", [P, PH, K])
        num = st.sb("num", [P, 2, SLOTS])
        zsum = st.sb("zsum", [P, PH])
        iota = st.sb("iota", [P, K])
        mark = st.sb("mark", [P, 1])
        pt = st.psum("pt", [P, 3, P])
        ahead = Ahead(core, st, A, 0, xh, xl)
        s_in = st.sem("s_in")
        iota_done = st.sem("iota_done")
        scores_used = st.sem("scores_used")
        ch = st.sem("chain")
        exp_in = st.sem("exp_in")
        exp_done = st.sem("exp_done")
        tile_done = st.sem("tile_done")
        turned = st.sem("turned")
        turned_read = st.sem("turned_read")
        block = st.block()

        @block.sync
        def _(sp):
            ahead.load(sp, 0)
            with sp.Fori(0, TILES) as t:
                for b in range(A):
                    ahead.load(sp, t * A + (b + 1))
                    ahead.store(sp, t * A + b)
            ahead.stored(sp, TILES * A)
            sp.wait_ge(ahead.u_in, 16 * (TILES * A + 1))

        @block.gpsimd
        def _(pool):
            nc.gpsimd.iota(iota[:], [[1, K]], base=0, channel_multiplier=0, allow_small_or_imprecise_dtypes=True)\
                .then_inc(iota_done, 1)
            with pool.Fori(0, TILES) as t:
                pool.wait_ge(scores_used, t + 1)
                pool.dma_start(s[:], dram["scores"][bass.ts(t, P), :].rearrange("t (h n) -> t h n", n=P)).then_inc(s_in, 16)

        @block.vector
        def _(dve):
            v = nc.vector
            TILE_COUNT = 1 + 16 + 32 + 16 + 16 + 8 + 8 + 16 + 8 + 8 + 5 + 3 + 2 * (1 + 8 + 1) + 2

            def tile(t):
                done = [0]

                def step(ins):
                    ins.then_inc(ch, 1)
                    done[0] += 1

                def meet():
                    dve.wait_ge(ch, t * TILE_COUNT + done[0])

                def link(ins):
                    step(ins)
                    meet()

                def rejoin():
                    meet()
                    step(v.memset(mark[:], 0.0))

                ahead.low(dve, t * A, 0)
                dve.wait_ge(s_in, 16 * (t + 1))
                step(v.memset(mark[:], 0.0))
                for j in range(HP):
                    step(v.max(sv[:, j // 2, j % 2, 0:8], s[:, j, :]))
                rejoin()
                for j in range(HP):
                    step(v.max_index(si[:, j // 2, j % 2, 0:8], sv[:, j // 2, j % 2, 0:8], s[:, j, :]))
                    step(v.match_replace(rest[:, j, :], sv[:, j // 2, j % 2, 0:8], s[:, j, :], LOWEST))
                meet()
                ahead.low(dve, t * A + 1, 1)
                for j in range(HP):
                    step(v.max(sv[:, j // 2, j % 2, 8:K], rest[:, j, :]))
                rejoin()
                for j in range(HP):
                    step(v.max_index(si[:, j // 2, j % 2, 8:K], sv[:, j // 2, j % 2, 8:K], rest[:, j, :]))
                meet()
                v.tensor_copy(sif[:], si[:]).then_inc(scores_used, 1)
                for h in range(PH):
                    step(v.tensor_tensor(cand[:, h], sv[:, h, 0, :].unsqueeze(2).to_broadcast([P, K, K]),
                                         sv[:, h, 1, :].unsqueeze(1).to_broadcast([P, K, K]), ALU.add))
                rejoin()
                c2 = lambda a, h: a[:, h].rearrange("p a b -> p (a b)")
                for h in range(PH):
                    step(v.max(cv[:, h, 0:8], c2(cand, h)))
                meet()
                ahead.low(dve, t * A + 2, 2)
                for h in range(PH):
                    step(v.max_index(ci[:, h, 0:8], cv[:, h, 0:8], c2(cand, h)))
                    step(v.match_replace(c2(crest, h), cv[:, h, 0:8], c2(cand, h), LOWEST))
                rejoin()
                for h in range(PH):
                    step(v.max(cv[:, h, 8:K], c2(crest, h)))
                rejoin()
                for h in range(PH):
                    step(v.max_index(ci[:, h, 8:K], cv[:, h, 8:K], c2(crest, h)))
                dve.wait_ge(turned, t + 1)
                v.tensor_tensor(gate[:], cv[:], cv[:, :, 0:1].to_broadcast([P, PH, K]), ALU.subtract).then_inc(exp_in, 1)
                meet()
                ahead.low(dve, t * A + 3, 3)
                step(v.tensor_scalar(part[:, 0], ci[:], 4, None, ALU.logical_shift_right))
                link(v.tensor_scalar(part[:, 1], ci[:], K - 1, None, ALU.bitwise_and))
                link(v.tensor_copy(partf[:], part[:]))
                dve.wait_ge(scores_used, t + 2)
                for half in range(2):
                    link(v.tensor_tensor(pick[:], partf[:, half].rearrange("p h k -> p (h k)").unsqueeze(2).to_broadcast([P, SLOTS, K]),
                                         iota[:].unsqueeze(1).to_broadcast([P, SLOTS, K]), ALU.is_equal))
                    p4 = pick[:].rearrange("p (h j) k -> p h j k", h=PH)
                    for h in range(PH):
                        step(v.tensor_tensor(p4[:, h], p4[:, h], sif[:, h, half, :].unsqueeze(1).to_broadcast([P, K, K]), ALU.mult))
                    meet()
                    link(v.tensor_reduce(num[:, half], pick[:], AX.X, ALU.add))
                    if half == 0:
                        ahead.low(dve, t * A + 4, 4)
                dve.wait_ge(exp_done, t + 1)
                link(v.tensor_reduce(zsum[:], gate[:], AX.X, ALU.add))
                link(v.reciprocal(zsum[:], zsum[:]))
                v.tensor_tensor(gate[:], gate[:], zsum[:].unsqueeze(2).to_broadcast([P, PH, K]), ALU.mult).then_inc(tile_done, 1)
                assert done[0] == TILE_COUNT

            dve.sem_inc(scores_used, 1)
            ahead.begin(dve=dve)
            dve.wait_ge(iota_done, 1)
            with dve.Fori(0, TILES) as t:
                tile(t)

        @block.scalar
        def _(act):
            def slots(t):
                act.wait_ge(turned, t + 2)
                nc.scalar.activation(core.slotT[:, :, bass.ts(t, P)], pt[:], ACT.Copy).then_inc(turned_read, 1)

            def others(t):
                for b in range(1, A - 1):
                    ahead.high(act, t * A + (b + 1), b + 1)
                    ahead.gelu(act, t * A + b)
                    if b == 2:
                        act.wait_ge(exp_in, t + 1)
                        nc.scalar.activation(gate[:], gate[:], ACT.Exp).then_inc(exp_done, 1)

            ahead.begin(act=act)
            act.sem_inc(turned_read, 1)
            ahead.high(act, 0, 0)
            ahead.high(act, 1, 1)
            ahead.gelu(act, 0)
            with act.Fori(0, TILES - 1) as t:
                others(t)
                ahead.high(act, t * A + A, 0)
                ahead.gelu(act, t * A + (A - 1))
                ahead.high(act, t * A + (A + 1), 1)
                ahead.gelu(act, t * A + A)
                slots(t)
            others(TILES - 1)
            ahead.gelu(act, TILES * A - 1)
            slots(TILES - 1)

        @block.tensor
        def _(pe):
            def first(t):
                for c in range(NTC):
                    ahead.products(pe, t * A, 0, c)

            def others(t):
                for b in range(1, A):
                    for c in range(NTC):
                        ahead.products(pe, t * A + b, b, c)

            def turn(t):
                pe.wait_ge(tile_done, t + 1)
                pe.wait_ge(turned_read, t + 1)
                nc.tensor.transpose(pt[:, 0, :], gate[:].rearrange("p h k -> p (h k)"), core.ident[:])
                for half in range(2):
                    last = nc.tensor.transpose(pt[:, 1 + half, :], num[:, half], core.ident[:])
                last.then_inc(turned, 1)

            ahead.begin(pe=pe)
            pe.sem_inc(turned, 1)
            first(0)
            with pe.Fori(0, TILES - 1) as t:
                others(t)
                first(t + 1)
                turn(t)
            others(TILES - 1)
            turn(TILES - 1)


def stage_gates(core, xh, xl):
    nc, dram = core.nc, core.dram
    TG = 4
    RING = 4
    HALF = P // 2
    BANKS = P // TG
    A = GATE_AHEAD
    PARTS = 4
    with Stage(core, "gates") as st:
        iota = st.sb("iota", [P, P])
        one = [st.sb(f"one{i}", [P, TG, P]) for i in range(RING)]
        scaled = [st.sb(f"scaled{i}", [P, TG, P]) for i in range(RING)]
        G = [st.sb(f"G{i}", [P, P, HALF]) for i in range(2)]
        pg = [st.psum(f"pg{i}", [P, TG, P]) for i in range(RING)]
        ahead = Ahead(core, st, A, TILES * TOPK_AHEAD, xh, xl)
        iota_done = st.sem("iota_done")
        hot = st.sem("hot")
        used = st.sem("used")
        read = st.sem("read")
        g_out = [st.sem(f"g_out{i}") for i in range(2)]
        block = st.block()

        @block.gpsimd
        def _(pool):
            nc.gpsimd.iota(iota[:], [[1, P]], base=0, channel_multiplier=0, allow_small_or_imprecise_dtypes=True)\
                .then_inc(iota_done, 1)

        @block.vector
        def _(dve):
            ahead.begin(dve=dve)
            dve.wait_ge(iota_done, 1)
            with dve.Fori(0, TILES) as t:
                for b in range(BANKS):
                    if b in (0, 12, 23):
                        ahead.low(dve, t * A + b // 11, b // 11)
                    i = b % RING
                    dve.wait_ge(used, t * BANKS + (b + 1))
                    for j in range(TG):
                        slot = lambda which: core.slotT[:, which, bass.ds(t * P + (b * TG + j), 1)]
                        nc.vector.tensor_scalar(one[i][:, j, :], iota[:], slot(2), None, ALU.is_equal)
                        last = nc.vector.tensor_scalar(scaled[i][:, j, :], iota[:], slot(1), slot(0), ALU.is_equal, ALU.mult)
                    last.then_inc(hot, 1)

        @block.tensor
        def _(pe):
            ahead.begin(pe=pe)
            pe.sem_inc(used, RING)
            with pe.Fori(0, TILES) as t:
                for b in range(BANKS):
                    i = b % RING
                    pe.wait_ge(hot, t * BANKS + (b + 1))
                    pe.wait_ge(read, t * BANKS + (b + 1))
                    for j in range(TG):
                        last = nc.tensor.matmul(pg[i][:, j, :], one[i][:, j, :], scaled[i][:, j, :], start=True, stop=True)
                    last.then_inc(used, 1)
                    if b % 2 == 1:
                        part = b // 2
                        ahead.products(pe, t * A + part // 6, part // 6, part // 2 % NTC, part % 2)
                ahead.products(pe, t * A + (A - 1), A - 1, NTC - 1)

        @block.scalar
        def _(act):
            ahead.begin(act=act)
            act.sem_inc(read, RING)
            act.sem_inc(g_out[0], 16 * PARTS)
            act.sem_inc(g_out[1], 16 * PARTS)
            ahead.high(act, 0, 0)
            with act.Fori(0, TILES) as t:
                for b in range(BANKS):
                    if b % (BANKS // 2) == 0:
                        act.wait_ge(g_out[b // (BANKS // 2)], 16 * PARTS * (t + 1))
                    half, at = b // (BANKS // 2), b % (BANKS // 2) * TG
                    act.wait_ge(used, t * BANKS + (b + 1 + RING))
                    nc.scalar.activation(G[half][:, :, at:at + TG], pg[b % RING][:].rearrange("p t i -> p i t"), ACT.Copy)\
                        .then_inc(read, 1)
                    if b % (BANKS // 2) == BANKS // 2 - 1:
                        act.wait_ge(read, t * BANKS + (b + 1 + RING))
                        for part in range(0, P, P // PARTS):
                            some = slice(part, part + P // PARTS)
                            dst = dram["gates"][some, :, bass.ds(t * P + half * HALF, HALF)].rearrange("a b t -> b a t")
                            act.dma_start(dst, G[half][:, some, :]).then_inc(g_out[half], 16)
                    if b in (4, 16, 28):
                        ahead.high(act, t * A + (b // 12 + 1), (b // 12 + 1) % A)
                    if b in (13, 25):
                        ahead.gelu(act, t * A + b // 14)
                        ahead.store(act, t * A + b // 14)
                ahead.gelu(act, t * A + (A - 1))
                ahead.store(act, t * A + (A - 1))
            ahead.stored(act, TILES * A)
            for i in range(2):
                act.wait_ge(g_out[i], 16 * PARTS * (TILES + 1))

        @block.sync
        def _(sp):
            ahead.load(sp, 0)
            with sp.Fori(0, TILES * A) as n:
                ahead.load(sp, n + 1)


def stage_stored(core, y, blocks):
    nc, dram = core.nc, core.dram
    PAIRS = blocks // 2
    NY, YC, RING = TILES * 2, D // 2, 6
    with Stage(core, "stored") as st:
        two = lambda name, shape, dt: [st.sb(f"{name}{i}", shape, dt) for i in range(2)]
        four = lambda name, shape, dt: [two(f"{name}{i}", shape, dt) for i in range(2)]
        Vr, C, G = two("Vr", [P, D], F32), two("C", [P, T], F32), two("G", [P, T], F32)
        Vh, Vl = four("Vh", [P, D], F32R), four("Vl", [P, D], F32R)
        Ch, Cl = four("Ch", [P, T], F32R), four("Cl", [P, T], F32R)
        pv = [st.psum(f"pv{i}", [P, YC]) for i in range(RING)]
        v_in = [st.sem(f"v_in{j}") for j in range(2)]
        c_in = [st.sem(f"c_in{j}") for j in range(2)]
        gated, c_high, v_high, c_split, v_split = (st.sem(n) for n in ("gated", "c_high", "v_high", "c_split", "v_split"))
        v_made, y_added, y_zero = st.sem("v_made"), st.sem("y_added"), st.sem("y_zero")
        block = st.block()

        def run(engine, prepare, use):
            prepare(0, 0)
            prepare(1, 1)
            use(0, 0)
            with engine.Fori(0, (PAIRS - 2) // 2) as i:
                for p in range(2):
                    prepare(2 * i + (2 + p), p)
                    use(2 * i + (1 + p), 1 - p)
            use(PAIRS - 1, 1)

        def is_(s, *values):
            return isinstance(s, int) and s in values

        nothing = lambda s, p: None

        @block.sync
        def _(sp):
            def load(s, p):
                for j in range(2):
                    if not is_(s, 0):
                        sp.wait_ge(c_split, 2 * s + (j - 1))
                    sp.dma_start(C[j][:], dram["acts"][2 * s + j]).then_inc(c_in[j], 16)
                    sp.dma_start(G[j][:], dram["gates"][2 * s + j]).then_inc(c_in[j], 16)
                for j in range(2):
                    if not is_(s, 0):
                        sp.wait_ge(v_split, 2 * s + (j - 1))
                    sp.dma_start(Vr[j][:], dram["peer_v"][2 * s + j]).then_inc(v_in[j], 16)

            run(sp, load, nothing)

        @block.gpsimd
        def _(pool):
            def gate(s, p):
                for j in range(2):
                    pool.wait_ge(c_in[j], 32 * (s + 1))
                    nc.gpsimd.tensor_tensor(C[j][:], C[j][:], G[j][:], ALU.mult).then_inc(gated, 1)

            run(pool, gate, nothing)

        @block.scalar
        def _(act):
            def high(s, p):
                if not is_(s, 0, 1):
                    act.wait_ge(v_made, NY * (s - 1))
                for j in range(2):
                    act.wait_ge(v_in[j], 16 * (s + 1))
                    nc.scalar.activation(Vh[p][j][:], Vr[j][:], ACT.Copy).then_inc(v_high, 1)
                    act.wait_ge(gated, 2 * s + (j + 1))
                    nc.scalar.activation(Ch[p][j][:], C[j][:], ACT.Copy).then_inc(c_high, 1)

            run(act, high, nothing)

        @block.vector
        def _(dve):
            def low_v(s, p, j):
                dve.wait_ge(v_high, 2 * s + (j + 1))
                nc.vector.tensor_tensor(Vl[p][j][:], Vr[j][:], Vh[p][j][:].bitcast(F32), ALU.subtract).then_inc(v_split, 1)

            def low_c(s, p, j):
                dve.wait_ge(c_high, 2 * s + (j + 1))
                nc.vector.tensor_tensor(Cl[p][j][:], C[j][:], Ch[p][j][:].bitcast(F32), ALU.subtract).then_inc(c_split, 1)

            def lows(s, p):
                for j in range(2):
                    low_v(s, p, j)
                    low_c(s, p, j)

            def add(s, p, ahead=True):
                for r in range(NY):
                    dve.wait_ge(v_made, NY * s + (r + 1))
                    if not is_(s, 0):
                        dve.wait_ge(y_added, NY * (s - 1) + (r + 1))
                    dst = y[:, r // 2, (r % 2) * YC:(r % 2 + 1) * YC]
                    nc.vector.tensor_tensor(dst, dst, pv[r % RING][:], ALU.add).then_inc(y_added, 1)
                    if ahead and r in (2, 9):
                        low_v(s + 1, 1 - p, r // 9)
                    if ahead and r in (6, 13):
                        low_c(s + 1, 1 - p, r // 13)

            nc.vector.memset(y[:], 0.0).then_inc(y_zero, 1)
            dve.wait_ge(y_zero, 1)
            lows(0, 0)
            add(0, 0)
            with dve.Fori(0, (PAIRS - 2) // 2) as i:
                add(2 * i + 1, 1)
                add(2 * i + 2, 0)
            add(PAIRS - 1, 1, ahead=False)

        @block.tensor
        def _(pe):
            mm = nc.tensor.matmul

            def use(s, p):
                pe.wait_ge(c_split, 2 * s + 2)
                pe.wait_ge(v_split, 2 * s + 2)
                for r in range(NY):
                    if not (is_(s, 0) and r < RING):
                        pe.wait_ge(y_added, NY * s + (r - RING + 1))
                    t, cols = slice(r // 2 * P, (r // 2 + 1) * P), slice((r % 2) * YC, (r % 2 + 1) * YC)
                    for j in range(2):
                        mm(pv[r % RING][:], Ch[p][j][:, t], Vh[p][j][:, cols], start=(j == 0), stop=False)
                        mm(pv[r % RING][:], Ch[p][j][:, t], Vl[p][j][:, cols], start=False, stop=False)
                        last = mm(pv[r % RING][:], Cl[p][j][:, t], Vh[p][j][:, cols], start=False, stop=(j == 1))
                    last.then_inc(v_made, 1)

            run(pe, nothing, use)


def stage_experts(core, xh, xl, y, first):
    nc, dram = core.nc, core.dram
    PAIRS = (P - first) // 2
    NY = TILES * 2
    YC = D // 2
    with Stage(core, "experts") as st:
        two = lambda name, shape, dt: [st.sb(f"{name}{i}", shape, dt) for i in range(2)]
        Ur, Uh, Ul = two("Ur", [P, KB, P], F32), two("Uh", [P, KB, P], F32R), two("Ul", [P, KB, P], F32R)
        Vr, Vh, Vl = two("Vr", [P, D], F32), two("Vh", [P, D], F32R), two("Vl", [P, D], F32R)
        G = two("G", [P, T], F32)
        tmp = [st.sb(f"tmp{c}", [P, TC], F32) for c in range(NTC)]
        Ch = [st.sb(f"Ch{i}", [P, T], F32R) for i in range(3)]
        Cl = [st.sb(f"Cl{i}", [P, T], F32R) for i in range(3)]
        pu = [st.psum(f"pu{c}", [P, 512]) for c in range(NTC)]
        pv = [st.psum(f"pv{i}", [P, YC]) for i in range(3)]
        u_in = [st.sem(f"u_in{j}") for j in range(2)]
        v_in = [st.sem(f"v_in{j}") for j in range(2)]
        g_in = [st.sem(f"g_in{j}") for j in range(2)]
        u_high, u_split, v_high, v_split = st.sem("u_high"), st.sem("u_split"), st.sem("v_high"), st.sem("v_split")
        u_made, gelu_done, gated, c_high, c_split = (st.sem(n) for n in ("u_made", "gelu_done", "gated", "c_high", "c_split"))
        v_made, y_added = st.sem("v_made"), st.sem("y_added")
        block = st.block()

        def run(engine, step):
            step(-1, 1)
            step(0, 0)
            with engine.Fori(0, (PAIRS - 4) // 2) as i:
                step(2 * i + 1, 1)
                step(2 * i + 2, 0)
            step(PAIRS - 3, 1)
            step(PAIRS - 2, 0)
            step(PAIRS - 1, 1)

        def is_(s, *values):
            return isinstance(s, int) and s in values

        def slot(parity, j):
            return 2 if j == 1 else 1 - parity

        @block.sync
        def _(sp):
            def load(b, j, what, fresh=False):
                if what == "u":
                    if not fresh:
                        sp.wait_ge(u_split, b - 1)
                    sp.dma_start(Ur[j][:], dram["peer_u"][b + first]).then_inc(u_in[j], 16)
                elif what == "v":
                    if not fresh:
                        sp.wait_ge(v_split, b - 1)
                    sp.dma_start(Vr[j][:], dram["peer_v"][b + first]).then_inc(v_in[j], 16)
                else:
                    if not fresh:
                        sp.wait_ge(gated, 3 * (b - 1))
                    sp.dma_start(G[j][:], dram["gates"][b + first]).then_inc(g_in[j], 16)

            for j in range(2):
                load(j, j, "u", True)
                load(j, j, "g", True)

            def step(s, parity):
                if is_(s, PAIRS - 1):
                    return
                for j in range(2):
                    load(2 * s + 2 + j, j, "v", is_(s, -1))
                if is_(s, PAIRS - 2):
                    return
                for j in range(2):
                    load(2 * s + 4 + j, j, "u")
                    load(2 * s + 4 + j, j, "g")

            run(sp, step)

        @block.scalar
        def _(act):
            def high_u(b, j, s):
                act.wait_ge(u_in[j], 16 * (s + 1))
                if not is_(b, 0, 1):
                    act.wait_ge(u_made, 3 * (b - 1))
                nc.scalar.activation(Uh[j][:], Ur[j][:], ACT.Copy).then_inc(u_high, 1)

            def coefficients(b, j, s, parity):
                def high(c):
                    act.wait_ge(gated, 3 * b + (c + 1))
                    nc.scalar.activation(Ch[slot(parity, j)][:, c * TC:(c + 1) * TC], tmp[c][:], ACT.Copy).then_inc(c_high, 1)

                if j == 0 and not is_(s, -1, 0):
                    act.wait_ge(v_made, NY * s)
                if j == 1 and not is_(s, -1):
                    act.wait_ge(v_made, NY * (s + 1))
                for c in range(NTC):
                    act.wait_ge(u_made, 3 * b + (c + 1))
                    if not is_(b, 0):
                        act.wait_ge(c_split, 3 * (b - 1) + (c + 1))
                    nc.scalar.activation(tmp[c][:], pu[c][:, 0:TC], ACT.Gelu_apprx_tanh).then_inc(gelu_done, 1)
                    if c > 0:
                        high(c - 1)
                high(NTC - 1)

            high_u(0, 0, 0)
            high_u(1, 1, 0)

            def step(s, parity):
                if is_(s, PAIRS - 1):
                    return
                coefficients(2 * s + 2, 0, s, parity)
                if not is_(s, PAIRS - 2):
                    high_u(2 * s + 4, 0, s + 2)
                if not is_(s, -1):
                    act.wait_ge(v_made, NY * (s + 1))
                for j in range(2):
                    act.wait_ge(v_in[j], 16 * (s + 2))
                    nc.scalar.activation(Vh[j][:], Vr[j][:], ACT.Copy).then_inc(v_high, 1)
                coefficients(2 * s + 3, 1, s, parity)
                if not is_(s, PAIRS - 2):
                    high_u(2 * s + 5, 1, s + 2)

            run(act, step)

        @block.vector
        def _(dve):
            sub = lambda low, raw, high: nc.vector.tensor_tensor(low, raw, high.bitcast(F32), ALU.subtract)

            def low_u(b, j):
                dve.wait_ge(u_high, b + 1)
                sub(Ul[j][:], Ur[j][:], Uh[j][:]).then_inc(u_split, 1)

            def coefficients(b, j, s, parity):
                def low(c):
                    dve.wait_ge(c_high, 3 * b + (c + 1))
                    i, cols = slot(parity, j), slice(c * TC, (c + 1) * TC)
                    sub(Cl[i][:, cols], tmp[c][:], Ch[i][:, cols]).then_inc(c_split, 1)

                dve.wait_ge(g_in[j], 16 * (s + 2))
                for c in range(NTC):
                    dve.wait_ge(gelu_done, 3 * b + (c + 1))
                    nc.vector.tensor_tensor(tmp[c][:], tmp[c][:], G[j][:, c * TC:(c + 1) * TC], ALU.mult).then_inc(gated, 1)
                    if c > 0:
                        low(c - 1)
                low(NTC - 1)

            low_u(0, 0)
            low_u(1, 1)

            def step(s, parity):
                if not is_(s, PAIRS - 1):
                    coefficients(2 * s + 2, 0, s, parity)
                    if not is_(s, PAIRS - 2):
                        low_u(2 * s + 4, 0)
                if not is_(s, -1):
                    for r in range(NY):
                        dve.wait_ge(v_made, NY * s + (r + 1))
                        if not is_(s, 0):
                            dve.wait_ge(y_added, NY * (s - 1) + (r + 1))
                        dst = y[:, r // 2, (r % 2) * YC:(r % 2 + 1) * YC]
                        nc.vector.tensor_tensor(dst, dst, pv[r % 3][:], ALU.add).then_inc(y_added, 1)
                if is_(s, PAIRS - 1):
                    return
                for j in range(2):
                    dve.wait_ge(v_high, 2 * s + (3 + j))
                    sub(Vl[j][:], Vr[j][:], Vh[j][:]).then_inc(v_split, 1)
                coefficients(2 * s + 3, 1, s, parity)
                if not is_(s, PAIRS - 2):
                    low_u(2 * s + 5, 1)

            run(dve, step)

        @block.tensor
        def _(pe):
            mm = nc.tensor.matmul

            def products_u(b, j):
                pe.wait_ge(u_split, b + 1)
                for c in range(NTC):
                    if not is_(b, 0):
                        pe.wait_ge(gelu_done, 3 * (b - 1) + (c + 1))
                    cols = slice(c * TC, (c + 1) * TC)
                    for k in range(KB):
                        mm(pu[c][:, 0:TC], Uh[j][:, k, :], xh[:, k, cols], start=(k == 0), stop=False)
                        mm(pu[c][:, 0:TC], Uh[j][:, k, :], xl[:, k, cols], start=False, stop=False)
                        last = mm(pu[c][:, 0:TC], Ul[j][:, k, :], xh[:, k, cols], start=False, stop=(k == KB - 1))
                    last.then_inc(u_made, 1)

            def products_v(s, parity):
                pe.wait_ge(c_split, 6 * s + 6)
                pe.wait_ge(v_split, 2 * s + 2)
                for r in range(NY):
                    if not (is_(s, 0) and r < 3):
                        pe.wait_ge(y_added, NY * s + (r - 2))
                    t, cols = r // 2, slice((r % 2) * YC, (r % 2 + 1) * YC)
                    t = slice(t * P, (t + 1) * P)
                    for j in range(2):
                        i = 2 if j == 1 else parity
                        mm(pv[r % 3][:], Ch[i][:, t], Vh[j][:, cols], start=(j == 0), stop=False)
                        mm(pv[r % 3][:], Ch[i][:, t], Vl[j][:, cols], start=False, stop=False)
                        last = mm(pv[r % 3][:], Cl[i][:, t], Vh[j][:, cols], start=False, stop=(j == 1))
                    last.then_inc(v_made, 1)

            def step(s, parity):
                if not is_(s, PAIRS - 1):
                    products_u(2 * s + 2, 0)
                if not is_(s, -1):
                    products_v(s, parity)
                if not is_(s, PAIRS - 1):
                    products_u(2 * s + 3, 1)

            run(pe, step)


def stage_final(core, y):
    nc, dram = core.nc, core.dram
    with Stage(core, "final") as st:
        gate = st.sb("gate", [P, GROUPS, D])
        x = [st.sb(f"x{i}", [P, D]) for i in range(3)]
        sq = st.sb("sq", [P, D])
        ss = st.sb("ss", [P, TILES])
        rstd = st.sb("rstd", [P, TILES])
        gate_spread = st.sem("gate_spread")
        gate_read = st.sem("gate_read")
        pg = [st.psum(f"pg{i}", [P, D]) for i in range(GROUPS)]
        x_in = [st.sem(f"x_in{i}") for i in range(3)]
        squared = st.sem("squared")
        mean_done = st.sem("mean_done")
        root_done = st.sem("root_done")
        ch = st.sem("chain")
        y_done = st.sem("y_done")
        y_out = st.sem("y_out")
        block = st.block()

        @block.sync
        def _(sp):
            for t in range(TILES):
                if t >= 3:
                    sp.wait_ge(y_done, t - 2)
                sp.dma_start(x[t % 3][:], dram["x1"][t * P:(t + 1) * P, :]).then_inc(x_in[t % 3], 16)

        @block.gpsimd
        def _(pool):
            for t in range(TILES):
                pool.wait_ge(y_done, t + 1)
                pool.dma_start(dram["y"][t * P:(t + 1) * P, :], y[:, t, :]).then_inc(y_out, 16)
            pool.wait_ge(y_out, 16 * TILES)

        @block.tensor
        def _(pe):
            for g in range(GROUPS):
                spread_gates(core, 1, pg[g], g).then_inc(gate_spread, 1)

        @block.scalar
        def _(act):
            for g in range(GROUPS):
                act.wait_ge(gate_spread, g + 1)
                nc.scalar.activation(gate[:, g, :], pg[g][:], ACT.Copy).then_inc(gate_read, 1)
            for t in range(TILES):
                if t > 0:
                    act.wait_ge(squared, t)
                nc.scalar.activation(sq[:], y[:, t, :], ACT.Square, accum_out=ss[:, t:t + 1]).then_inc(squared, 1)
            act.wait_ge(mean_done, 1)
            nc.scalar.activation(ss[:], rstd[:], ACT.Sqrt).then_inc(root_done, 1)

        @block.vector
        def _(dve):
            link = Chain(dve, ch)
            dve.wait_ge(squared, TILES)
            nc.vector.tensor_scalar(rstd[:], ss[:], 1.0 / D, EPS, ALU.mult, ALU.add).then_inc(mean_done, 1)
            dve.wait_ge(root_done, 1)
            link(nc.vector.reciprocal(rstd[:], ss[:]))
            dve.wait_ge(gate_read, GROUPS)
            for t in range(TILES):
                link(nc.vector.scalar_tensor_tensor(out=y[:, t, :], in0=y[:, t, :], scalar=rstd[:, t:t + 1],
                                                    in1=gate[:, group_of(t), :], op0=ALU.mult, op1=ALU.mult))
                dve.wait_ge(x_in[t % 3], 16 * (t // 3 + 1))
                nc.vector.tensor_tensor(y[:, t, :], y[:, t, :], x[t % 3][:], ALU.add).then_inc(y_done, 1)


def build(nc, dram):
    dram["x1"] = nc.dram_tensor("x1", (T, D), F32).ap()
    dram["scores"] = nc.dram_tensor("scores", (T, 2 * PH * P), F32).ap()
    dram["gates"] = nc.dram_tensor("gates", (P, P, T), F32).ap()
    dram["acts"] = nc.dram_tensor("acts", (P, P, T), F32).ap()
    with ExitStack() as stack:
        core = Core(nc, dram, stack)
        core.ident = core.keep("ident", [P, P])
        core.ones = core.keep("ones", [P, P])
        core.tri = core.keep("tri", [P, 2, P])
        core.shift_cols = core.keep("shift_cols", [P, 2, KB, GROUPS])
        core.scale_cols = core.keep("scale_cols", [P, 2, KB, GROUPS])
        core.gate_cols = core.keep("gate_cols", [P, 2, KB, GROUPS])
        core.cact = core.keep("cact", [P, KB, GROUPS])
        stage_modulation(core)
        with Stage(core, "mixer") as mx:
            core.hT = mx.sb("hT", [P, KB, T])
            stage_norm(core, "norm1", dram["x"], 0)
            out = {n: mx.sb(n, [P, TILES, HW]) for n in ("q", "k", "v", "z")}
            out["guT"] = mx.sb("guT", [P, HEADS, T])
            for n in ("g", "beta", "neg_cum", "exp_cum", "exp_rest", "exp_tot"):
                out[n] = mx.sb(n, [P, TILES, UNITS])
            with Stage(core, "front") as fr:
                out["ab"] = fr.sb("ab", [P, TILES, 2 * UNITS])
                out["gv"] = fr.sb("gv", [P, TILES, HW])
                stage_project(core, out)
                stage_gmlp(core, out)
                stage_prepare(core, out)
            stage_scan(core, out)
            stage_out(core, out)
        core.recycle_semaphores()
        with Stage(core, "peer") as pr:
            xh = pr.sb("xh", [P, KB, T], F32R)
            xl = pr.sb("xl", [P, KB, T], F32R)
            with Stage(core, "h2") as h2:
                core.hT = h2.sb("hT", [P, KB, T])
                stage_norm(core, "norm2", dram["x1"], 1)
                stage_queries(core, core.hT, xh, xl)
            with Stage(core, "retrieve") as rt:
                core.slotT = rt.sb("slotT", [P, 3, T])
                stage_topk(core, xh, xl)
                stage_gates(core, xh, xl)
            y = pr.sb("y", [P, TILES, D])
            made = TILES * (TOPK_AHEAD + GATE_AHEAD)
            stage_stored(core, y, made)
            stage_experts(core, xh, xl, y, made)
            stage_final(core, y)


def constants():
    i = np.arange(P)
    tri = np.stack([i[:, None] <= i[None, :], i[:, None] >= i[None, :]], 1).astype(np.float32)
    far = np.stack([np.where(i[:, None] <= i[None, :], 0.0, FAR), np.where(i[:, None] >= i[None, :], 0.0, FAR)], 1)
    level = np.zeros((P, 2, LEVELS, P), np.float32)
    for l in range(LEVELS):
        b = 1 << l
        same = (i[:, None] // (2 * b)) == (i[None, :] // (2 * b))
        first = (i[:, None] // b) % 2 == 0
        level[:, 0, l] = same & first & ((i[None, :] // b) % 2 == 1)
        level[:, 1, l] = same & ~first & ((i[None, :] // b) % 2 == 0)
    n = np.arange((TILES - 1) * P)
    inv = (np.float32(10000.0) ** (-np.arange(32, dtype=np.float32) / np.float32(32))).astype(np.float32)
    row = (n // 64).astype(np.float32)[:, None] * inv
    col = (n % 64).astype(np.float32)[:, None] * inv
    cos = np.concatenate([np.cos(row), np.cos(row), np.cos(col), np.cos(col)], 1)
    sin = np.concatenate([-np.sin(row), np.sin(row), -np.sin(col), np.sin(col)], 1)
    tok = lambda a: np.ascontiguousarray(a.astype(np.float32).reshape(TILES - 1, P, P).transpose(1, 0, 2))
    return {"tri": tri, "far_masks": far.astype(np.float32), "level_masks": level, "rope_cos": tok(cos), "rope_sin": tok(sin)}


def lay_out(i):
    a = {k: np.asarray(v) for k, v in i.items()}
    blocks = lambda w: w.reshape(-1, P, w.shape[-1]).transpose(1, 0, 2)
    cols = lambda v: v.reshape(-1, P).T
    d = {}
    d["x"] = np.concatenate([a["x_prompt"].reshape(-1, D), a["x_sample"].reshape(-1, D)])
    d["c_cols"] = np.stack([cols(a["c_ctx"]), cols(a["c"][0])], 2)
    d["w_mod"] = blocks(a["w_mod"][0])
    b = a["b_mod"][0]
    d["b_mod_cols"] = cols(b)
    gains = [a[n][0] for n in ("g_pre_mix", "g_pre_ffn", "g_post_mix", "g_post_ffn")]
    d["gain_cols"] = np.stack([cols(g) for g in gains], 1).reshape(P, 2, 2, KB)
    d["w_in"] = blocks(a["w_in"][0])
    d["w_out"] = blocks(a["w_out"][0])
    d["gm_ws"] = a["gm_ws"][0].transpose(2, 0, 1)
    d["gm_bs"] = a["gm_bs"][0]
    d["conv_taps"] = a["dn_conv"][0].reshape(3, 12, P).transpose(2, 0, 1)
    d["decay_rows"] = np.stack([a["dn_a_log"][0].reshape(-1), a["dn_dt_bias"][0].reshape(-1)])
    d["norm_row"] = a["dn_norm"][0]
    d["state"] = a["state_delta"][0, 0].transpose(0, 2, 1, 3)
    d["peer_wq"] = blocks(a["peer_wq"][0])
    d["peer_keys"] = a["peer_keys"][0].reshape(2 * PH, P, P).transpose(2, 0, 1)
    d["peer_u"] = a["peer_u"][0].reshape(P, P, KB, P).transpose(0, 3, 2, 1)
    d["peer_v"] = a["peer_v"][0].reshape(P, P, D)
    d.update(constants())
    return {k: np.ascontiguousarray(v) for k, v in d.items()}


def kernel(**inputs):
    import concourse.bacc as bacc
    from concourse.bass_utils import run_bass_kernel_spmd

    nc = bacc.Bacc("TRN2", target_bir_lowering=False, num_devices=1)
    arrays = {f"in_{n}": a for n, a in lay_out(inputs).items()}
    dram = {n[3:]: nc.dram_tensor(n, a.shape, F32, kind="ExternalInput").ap() for n, a in arrays.items()}
    for n in ("gm_bs", "decay_rows"):
        dram[n] = dram[n].unsqueeze(0)
    dram["norm_row"] = dram["norm_row"].unsqueeze(0)
    dram["y"] = nc.dram_tensor("out_y", (T, D), F32, kind="ExternalOutput").ap()
    dram["new_state"] = nc.dram_tensor("out_state", (2, P, HEADS, P), F32, kind="ExternalOutput").ap()
    build(nc, dram)
    r = run_bass_kernel_spmd(nc, [arrays], core_ids=[0]).results[0]
    y = r["out_y"]
    state = r["out_state"].transpose(0, 2, 1, 3)
    return (np.ascontiguousarray(y[:P].reshape(1, P, D)), np.ascontiguousarray(y[P:].reshape(1, T - P, D)),
            np.ascontiguousarray(state.reshape(1, 1, 2, HEADS, P, P)))
```
